# Optimizing a Trainium2 kernel written in Bass

```python
import jax, jax.numpy as jnp
from jax import lax
import numpy as np

D_MODEL = 2048
BATCH = 1
SEQ = 256
DEPTH = 1

GRID_W = 64
WIN_R = 8
WIN_C = 16
ATTN_HEADS = 8
HEAD_DIM = 128
D_ATTN = ATTN_HEADS * HEAD_DIM
D_CONV = D_MODEL // 2
CONV_WIDTH = 31
CONV_PAD = CONV_WIDTH // 2
D_FF = -(-8 * D_MODEL // (3 * 256)) * 256
EPS = 1e-6
IN_SPLITS = [D_ATTN, D_ATTN, D_ATTN, D_CONV, D_CONV, D_MODEL, D_MODEL]
N_IN = sum(IN_SPLITS)


def rms_norm(x, g):
    xf = x.astype(jnp.float32)
    y = xf * lax.rsqrt(jnp.mean(xf * xf, axis=-1, keepdims=True) + EPS) * g.astype(jnp.float32)
    return y.astype(x.dtype)

def layer_norm(x, g, b):
    xf = x.astype(jnp.float32)
    mu = jnp.mean(xf, axis=-1, keepdims=True)
    xc = xf - mu
    var = jnp.mean(xc * xc, axis=-1, keepdims=True)
    y = xc * lax.rsqrt(var + EPS) * g.astype(jnp.float32) + b.astype(jnp.float32)
    return y.astype(x.dtype)

def neighbourhood_attention(q, k, v, rpb):
    B, S, H, Dh = q.shape
    rows = S // GRID_W
    kr = min(WIN_R, rows)
    kc = min(WIN_C, GRID_W)
    qg = q.reshape(B, rows, GRID_W, H, Dh)
    kg = k.reshape(B, rows, GRID_W, H, Dh)
    vg = v.reshape(B, rows, GRID_W, H, Dh)
    col = jnp.arange(GRID_W)
    col_start = jnp.clip(col - kc // 2, 0, GRID_W - kc)
    col_idx = col_start[:, None] + jnp.arange(kc)[None, :]
    dc = col_idx - col[:, None]
    rpb_cols = rpb[:, :, dc + WIN_C - 1]
    scale = HEAD_DIM ** -0.5

    def one_row(r):
        r_start = jnp.clip(r - kr // 2, 0, rows - kr)
        kb = lax.dynamic_slice_in_dim(kg, r_start, kr, axis=1)
        vb = lax.dynamic_slice_in_dim(vg, r_start, kr, axis=1)
        kw = kb[:, :, col_idx]
        vw = vb[:, :, col_idx]
        qr = lax.dynamic_index_in_dim(qg, r, axis=1, keepdims=False)
        s = jnp.einsum('bwhd,biwjhd->bhwij', qr, kw).astype(jnp.float32) * scale
        dr = r_start + jnp.arange(kr) - r
        bias = jnp.transpose(rpb_cols[:, dr + WIN_R - 1], (0, 2, 1, 3))
        s = s + bias[None].astype(jnp.float32)
        p = jax.nn.softmax(s.reshape(B, H, GRID_W, kr * kc), axis=-1)
        p = p.reshape(B, H, GRID_W, kr, kc).astype(vw.dtype)
        return jnp.einsum('bhwij,biwjhd->bwhd', p, vw)

    out = lax.map(one_row, jnp.arange(rows))
    return jnp.transpose(out, (1, 0, 2, 3, 4)).reshape(B, S, H * Dh)

def conformer_conv(a, b, w_dw, b_dw, ln_g, ln_b, w_pw):
    z = a * jax.nn.sigmoid(b)
    z = lax.conv_general_dilated(
        z, w_dw[:, None, :].astype(z.dtype), window_strides=(1,),
        padding=[(CONV_PAD, CONV_PAD)],
        dimension_numbers=('NWC', 'WIO', 'NWC'),
        feature_group_count=z.shape[-1]) + b_dw
    z = layer_norm(z, ln_g, ln_b)
    z = jax.nn.silu(z)
    return z @ w_pw

def first_inputs(seed: int = 0) -> dict:
    key = jax.random.key(seed)
    ks = jax.random.split(key, 20)
    f32 = jnp.float32
    nrm = lambda k, shape, s: jax.random.normal(k, shape, f32) * s
    gain = lambda k, n: 1.0 + 0.05 * jax.random.normal(k, (DEPTH, n), f32)
    return {
        'x': jax.random.normal(ks[0], (BATCH, SEQ, D_MODEL), f32),
        'mix_pre_g': gain(ks[1], D_MODEL),
        'mix_post_g': gain(ks[2], D_MODEL),
        'w_in': nrm(ks[3], (DEPTH, D_MODEL, N_IN), D_MODEL ** -0.5),
        'rpb': nrm(ks[4], (DEPTH, ATTN_HEADS, 2 * WIN_R - 1, 2 * WIN_C - 1), 0.1),
        'w_attn_o': nrm(ks[5], (DEPTH, D_ATTN, D_MODEL), D_ATTN ** -0.5),
        'w_dw': nrm(ks[6], (DEPTH, CONV_WIDTH, D_CONV), CONV_WIDTH ** -0.5),
        'b_dw': nrm(ks[7], (DEPTH, D_CONV), 0.02),
        'conv_ln_g': gain(ks[8], D_CONV),
        'conv_ln_b': nrm(ks[9], (DEPTH, D_CONV), 0.02),
        'w_conv_o': nrm(ks[10], (DEPTH, D_CONV, D_MODEL), D_CONV ** -0.5),
        'w_out': nrm(ks[11], (DEPTH, D_MODEL, D_MODEL), D_MODEL ** -0.5),
        'ffn_pre_g': gain(ks[12], D_MODEL),
        'ffn_post_g': gain(ks[13], D_MODEL),
        'w_gate_up': nrm(ks[14], (DEPTH, D_MODEL, 2 * D_FF), D_MODEL ** -0.5),
        'w_down': nrm(ks[15], (DEPTH, D_FF, D_MODEL), D_FF ** -0.5),
    }

def first_block(x, mix_pre_g, mix_post_g, w_in, rpb, w_attn_o, w_dw, b_dw,
              conv_ln_g, conv_ln_b, w_conv_o, w_out, ffn_pre_g, ffn_post_g,
              w_gate_up, w_down):
    B, S, D = x.shape
    split_pts = list(np.cumsum(IN_SPLITS)[:-1])
    h = x
    for l in range(DEPTH):
        u = rms_norm(h, mix_pre_g[l])
        proj = u @ w_in[l]
        q, k, v, ca, cb, ga, gb = jnp.split(proj, split_pts, axis=-1)
        q = q.reshape(B, S, ATTN_HEADS, HEAD_DIM)
        k = k.reshape(B, S, ATTN_HEADS, HEAD_DIM)
        v = v.reshape(B, S, ATTN_HEADS, HEAD_DIM)
        y_attn = neighbourhood_attention(q, k, v, rpb[l]) @ w_attn_o[l]
        y_conv = conformer_conv(ca, cb, w_dw[l], b_dw[l], conv_ln_g[l],
                                conv_ln_b[l], w_conv_o[l])
        merged = jax.nn.sigmoid(ga) * y_attn + jax.nn.sigmoid(gb) * y_conv
        h = h + rms_norm(merged @ w_out[l], mix_post_g[l])
        u = rms_norm(h, ffn_pre_g[l])
        gate, up = jnp.split(u @ w_gate_up[l], 2, axis=-1)
        f = (jax.nn.silu(gate) * up) @ w_down[l]
        h = h + rms_norm(f, ffn_post_g[l])
    return h


MIX_WIDTH = D_MODEL
DSWA_HEADS = (MIX_WIDTH // 2) // HEAD_DIM
DSWA_CONFIGS = ((128, 1), (512, 4), (2048, 16))
ROT_DIM = HEAD_DIM // 4
ROPE_THETA = 500000.0
MLA_HEADS = (MIX_WIDTH // 2) // HEAD_DIM
Q_LORA_RANK = 512
KV_LORA_RANK = 512
QK_NOPE_DIM = 128
QK_ROPE_DIM = 64
V_HEAD_DIM = 128
D_FF_2 = 4 * D_MODEL
Q_BLOCK = 128
NORM_EPS = 1e-6
NEG_INF = -1e30

A_WIDTH = DSWA_HEADS * HEAD_DIM
IN_SPLITS_2 = (A_WIDTH, 2 * A_WIDTH, 3 * A_WIDTH,
             3 * A_WIDTH + Q_LORA_RANK,
             3 * A_WIDTH + Q_LORA_RANK + KV_LORA_RANK)
IN_COLS = 3 * A_WIDTH + Q_LORA_RANK + KV_LORA_RANK + QK_ROPE_DIM
OUT_ROWS = DSWA_HEADS * HEAD_DIM + MLA_HEADS * V_HEAD_DIM


def _rmsnorm(x, gain):
    xf = x.astype(jnp.float32)
    xf = xf * lax.rsqrt(jnp.mean(xf * xf, axis=-1, keepdims=True) + NORM_EPS)
    return xf.astype(x.dtype) * gain

def _rope(x, positions, rot_dim):
    inv_freq = ROPE_THETA ** (-jnp.arange(0, rot_dim, 2, dtype=jnp.float32) / rot_dim)
    ang = positions.astype(jnp.float32)[..., None] * inv_freq
    cos = jnp.cos(ang)[:, :, None, :]
    sin = jnp.sin(ang)[:, :, None, :]
    xr = x[..., :rot_dim].astype(jnp.float32)
    x1, x2 = xr[..., : rot_dim // 2], xr[..., rot_dim // 2:]
    rot = jnp.concatenate([x1 * cos - x2 * sin, x2 * cos + x1 * sin], axis=-1)
    return jnp.concatenate([rot.astype(x.dtype), x[..., rot_dim:]], axis=-1)

def _dilated_window_attention(q, k, v, window, dilation):
    B, S, H, D = q.shape
    steps = window // dilation
    span = dilation * Q_BLOCK
    s_pad = -(-S // span) * span
    pad = ((0, 0), (0, s_pad - S), (0, 0), (0, 0))
    q, k, v = jnp.pad(q, pad), jnp.pad(k, pad), jnp.pad(v, pad)
    nb = s_pad // span
    qb = q.reshape(B, nb, Q_BLOCK, dilation, H, D)
    kb = k.reshape(B, nb, Q_BLOCK, dilation, H, D)
    vb = v.reshape(B, nb, Q_BLOCK, dilation, H, D)

    def with_prev(t):
        prev = jnp.pad(t[:, :-1], ((0, 0), (1, 0), (0, 0), (0, 0), (0, 0), (0, 0)))
        return jnp.concatenate([prev, t], axis=2)

    kc, vc = with_prev(kb), with_prev(vb)
    s = jnp.einsum('bniphd,bnjphd->bnphij', qb, kc).astype(jnp.float32) * (D ** -0.5)
    i = jnp.arange(Q_BLOCK)[:, None]
    j = jnp.arange(2 * Q_BLOCK)[None, :]
    dist = i + Q_BLOCK - j
    band = (dist >= 0) & (dist <= steps)
    first = (jnp.arange(nb) == 0)[:, None, None] & (j < Q_BLOCK)[None]
    mask = band[None] & ~first
    s = jnp.where(mask[None, :, None, None], s, NEG_INF)
    m = jnp.max(s, axis=-1, keepdims=True)
    p = jnp.exp(s - m)
    denom = jnp.sum(p, axis=-1, keepdims=True)
    o = jnp.einsum('bnphij,bnjphd->bniphd', (p / denom).astype(v.dtype), vc)
    lse = (m + jnp.log(denom))[..., 0]
    o = o.reshape(B, s_pad, H, D)[:, :S]
    lse = jnp.transpose(lse, (0, 1, 4, 2, 3)).reshape(B, s_pad, H)[:, :S]
    return o, lse

def _causal_block_attention(q, k, v, scale):
    B, S, H, Dk = q.shape
    nb = S // Q_BLOCK
    qb = q.reshape(B, nb, Q_BLOCK, H, Dk).transpose(1, 0, 2, 3, 4)
    key_pos = jnp.arange(S)

    def one_block(args):
        n, qn = args
        s = jnp.einsum('bqhd,bkhd->bhqk', qn, k).astype(jnp.float32) * scale
        q_pos = n * Q_BLOCK + jnp.arange(Q_BLOCK)
        s = jnp.where((key_pos[None, :] <= q_pos[:, None])[None, None], s, NEG_INF)
        p = jax.nn.softmax(s, axis=-1)
        return jnp.einsum('bhqk,bkhd->bqhd', p.astype(v.dtype), v)

    o = lax.map(one_block, (jnp.arange(nb), qb))
    return o.transpose(1, 0, 2, 3, 4).reshape(B, S, H, v.shape[-1])

def second_inputs(seed: int = 0) -> dict:
    key = jax.random.key(seed)
    ks = jax.random.split(key, 16)
    f32 = jnp.float32

    def w(k, shape, fan_in):
        return jax.random.normal(k, shape, f32) * (fan_in ** -0.5)

    def gain(k, n):
        return 1.0 + 0.05 * jax.random.normal(k, (DEPTH, n), f32)

    x = jax.random.normal(ks[0], (BATCH, SEQ, D_MODEL), f32)
    offset = jax.random.randint(ks[1], (BATCH, 1), 0, 2048, dtype=jnp.int32)
    positions = offset + jnp.arange(SEQ, dtype=jnp.int32)[None, :]
    return {
        "x": x,
        "positions": positions,
        "norm_attn_pre": gain(ks[2], D_MODEL),
        "norm_attn_post": gain(ks[3], D_MODEL),
        "w_in": w(ks[4], (DEPTH, D_MODEL, IN_COLS), D_MODEL),
        "q_latent_norm": gain(ks[5], Q_LORA_RANK),
        "kv_latent_norm": gain(ks[6], KV_LORA_RANK),
        "w_uq": w(ks[7], (DEPTH, Q_LORA_RANK, MLA_HEADS * (QK_NOPE_DIM + QK_ROPE_DIM)), Q_LORA_RANK),
        "w_ukv": w(ks[8], (DEPTH, KV_LORA_RANK, MLA_HEADS * (QK_NOPE_DIM + V_HEAD_DIM)), KV_LORA_RANK),
        "w_out": w(ks[9], (DEPTH, OUT_ROWS, D_MODEL), OUT_ROWS),
        "norm_mlp_pre": gain(ks[10], D_MODEL),
        "norm_mlp_post": gain(ks[11], D_MODEL),
        "w_up": w(ks[12], (DEPTH, D_MODEL, D_FF_2), D_MODEL),
        "w_down": w(ks[13], (DEPTH, D_FF_2, D_MODEL), D_FF_2),
    }

def second_block(x, positions, norm_attn_pre, norm_attn_post, w_in, q_latent_norm,
              kv_latent_norm, w_uq, w_ukv, w_out, norm_mlp_pre, norm_mlp_post,
              w_up, w_down):
    B, S, _ = x.shape
    for layer in range(DEPTH):
        h = _rmsnorm(x, norm_attn_pre[layer])
        proj = h @ w_in[layer]
        a_q, a_k, a_v, c_q, c_kv, k_r = jnp.split(proj, IN_SPLITS_2, axis=-1)

        a_q = _rope(a_q.reshape(B, S, DSWA_HEADS, HEAD_DIM), positions, ROT_DIM)
        a_k = _rope(a_k.reshape(B, S, DSWA_HEADS, HEAD_DIM), positions, ROT_DIM)
        a_v = a_v.reshape(B, S, DSWA_HEADS, HEAD_DIM)
        outs, lses = [], []
        for window, dilation in DSWA_CONFIGS:
            o, lse = _dilated_window_attention(a_q, a_k, a_v, window, dilation)
            outs.append(o)
            lses.append(lse)
        alpha = jax.nn.softmax(jnp.stack(lses, axis=0), axis=0)
        a_out = jnp.sum(alpha[..., None].astype(a_v.dtype) * jnp.stack(outs, axis=0), axis=0)

        c_q = _rmsnorm(c_q, q_latent_norm[layer])
        q_b = (c_q @ w_uq[layer]).reshape(B, S, MLA_HEADS, QK_NOPE_DIM + QK_ROPE_DIM)
        q_nope, q_rope = q_b[..., :QK_NOPE_DIM], q_b[..., QK_NOPE_DIM:]
        q_rope = _rope(q_rope, positions, QK_ROPE_DIM)
        c_kv = _rmsnorm(c_kv, kv_latent_norm[layer])
        kv = (c_kv @ w_ukv[layer]).reshape(B, S, MLA_HEADS, QK_NOPE_DIM + V_HEAD_DIM)
        k_nope, v_b = kv[..., :QK_NOPE_DIM], kv[..., QK_NOPE_DIM:]
        k_rope = _rope(k_r[:, :, None, :], positions, QK_ROPE_DIM)
        q_full = jnp.concatenate([q_nope, q_rope], axis=-1)
        k_full = jnp.concatenate(
            [k_nope, jnp.broadcast_to(k_rope, (B, S, MLA_HEADS, QK_ROPE_DIM))], axis=-1)
        b_out = _causal_block_attention(q_full, k_full, v_b,
                                        (QK_NOPE_DIM + QK_ROPE_DIM) ** -0.5)

        mixed = jnp.concatenate([a_out.reshape(B, S, DSWA_HEADS * HEAD_DIM),
                                 b_out.reshape(B, S, MLA_HEADS * V_HEAD_DIM)], axis=-1)
        x = x + _rmsnorm(mixed @ w_out[layer], norm_attn_post[layer])

        h = _rmsnorm(x, norm_mlp_pre[layer])
        u = jnp.square(jax.nn.relu(h @ w_up[layer]))
        x = x + _rmsnorm(u @ w_down[layer], norm_mlp_post[layer])
    return x


def setup_inputs(seed=0):
    out = dict(first_inputs(seed))
    for name, value in second_inputs(seed + 1).items():
        if name != "x":
            out[name + "_2"] = value
    return out


def reference(
    x, mix_pre_g, mix_post_g, w_in, rpb, w_attn_o, w_dw, b_dw, conv_ln_g, conv_ln_b, w_conv_o,
    w_out, ffn_pre_g, ffn_post_g, w_gate_up, w_down, positions_2, norm_attn_pre_2,
    norm_attn_post_2, w_in_2, q_latent_norm_2, kv_latent_norm_2, w_uq_2, w_ukv_2, w_out_2,
    norm_mlp_pre_2, norm_mlp_post_2, w_up_2, w_down_2,
):
    x = first_block(
        x, mix_pre_g, mix_post_g, w_in, rpb, w_attn_o, w_dw, b_dw, conv_ln_g, conv_ln_b,
        w_conv_o, w_out, ffn_pre_g, ffn_post_g, w_gate_up, w_down,
    )
    return second_block(
        x, positions_2, norm_attn_pre_2, norm_attn_post_2, w_in_2, q_latent_norm_2,
        kv_latent_norm_2, w_uq_2, w_ukv_2, w_out_2, norm_mlp_pre_2, norm_mlp_post_2, w_up_2,
        w_down_2,
    )


_drawn_inputs = setup_inputs


def setup_inputs(seed=0):
    import zlib

    import numpy as np

    out = dict(_drawn_inputs(seed))
    spreads = {}
    factors = {'q_latent_norm_2': 5.379, 'kv_latent_norm_2': 2.881}
    for name, (base, spread) in spreads.items():
        noise = np.random.default_rng([zlib.crc32(name.encode()), seed]).standard_normal(out[name].shape)
        drawn = base * np.exp(spread * noise) if base else spread * noise
        out[name] = __import__('jax').numpy.asarray(drawn.astype(out[name].dtype))
    for name, factor in factors.items():
        out[name] = (out[name] * factor).astype(out[name].dtype)
    return out
```

```python
from contextlib import ExitStack

import concourse.bass as bass
from concourse import mybir

F32 = mybir.dt.float32
F32R = mybir.dt.float32r
I32 = mybir.dt.int32
ACT = mybir.ActivationFunctionType
ALU = mybir.AluOpType
AX_X = mybir.AxisListType.X

P = 128
T = 256
D = 2048
H = 8
DH = 128
D_CONV = 1024
TAPS = 31
PAD = TAPS // 2
D_FF = 5632
D_FF2 = 8192
RANK = 512
ROPE_A = 32
ROPE_B = 64
EPS = 1e-6
N = 512
AHEAD = 4
SCALE_A = DH ** -0.5
SCALE_B = (DH + ROPE_B) ** -0.5

STAGES = [("conv_in", 2, 16), ("qkv", 3, 16), ("gates", 4, 16), ("merge", 4, 8), ("out1", 2, 16),
          ("ff1", 11, 16), ("down1", 2, 44), ("latent", 1, 16), ("krope", 1, 1), ("aqkv", 3, 16),
          ("up_lat", 7, 2), ("out2", 2, 16), ("up2a", 4, 16), ("down2a", 2, 32), ("up2b", 4, 16),
          ("down2b", 2, 32)]
C0 = {}
TOTAL = 0
for _name, _pairs, _per in STAGES:
    C0[_name] = TOTAL
    TOTAL += _pairs * _per

A0, B0 = {}, {}
_a = _b = 0
for _name, _na, _nb in [("conv_in", 0, 2), ("qkv", 3, 3), ("gates", 4, 4), ("merge", 4, 0), ("out1", 1, 1),
                        ("ff1", 11, 0), ("down1", 1, 1), ("latent", 0, 0), ("aqkv", 3, 3), ("up_lat", 4, 3),
                        ("out2", 1, 1), ("up2a", 4, 4), ("down2a", 2, 2), ("up2b", 4, 4), ("down2b", 2, 2)]:
    A0[_name], B0[_name] = _a, _b
    _a += _na
    _b += _nb

_sums = [("x", 8), ("out1", 8), ("h1", 8), ("down1", 8), ("h2", 8), ("latent", 4), ("out2", 8), ("h3", 8),
         ("down2", 8)]
SUMS = {n: sum(k for _, k in _sums[:i + 1]) for i, (n, _) in enumerate(_sums)}

ORDER = [2, 3, 0, 1]
PERM = [2 * q + i for q in ORDER for i in range(2)]

G0 = {"x": 0, "z": 4, "merged": 6, "h1": 10, "f": 14, "h2": 25, "latent": 29, "h3": 31, "u0": 35, "u1": 43,
      "end": 51}

GAINS = [("mix_pre_g", 16), ("ffn_pre_g", 16), ("norm_attn_pre_2", 16), ("norm_mlp_pre_2", 16),
         ("q_latent_norm_2", 4), ("kv_latent_norm_2", 4), ("conv_ln_g", 8), ("conv_ln_b", 8), ("b_dw", 8)]
GC = {}
_c = 0
for _name, _n in GAINS:
    GC[_name] = _c
    _c += _n
NGAIN = _c

TWO_PI = 6.283185307179586
PI_LO = 3.1415925


def build(nc, a, out):
    ctx = ExitStack()

    def sb(name, shape, dt=F32, c=ctx):
        return c.enter_context(nc.sbuf_tensor(name, shape, dt))

    def sem(name):
        return ctx.enter_context(nc.semaphore(name))

    raw = sb("raw", [P, 4, 1024])
    hi = sb("hi", [P, 4, 1024], F32R)
    lo = sb("lo", [P, 4, 1024], F32R)
    xh = sb("xh", [P, 16, T], F32R)
    xl = sb("xl", [P, 16, T], F32R)
    st = sb("st", [P, 2, 2, N])
    sg = sb("sg", [P, 2, N])
    ident = sb("ident", [P, P])
    ones = sb("ones", [P, P])
    gcol = sb("gcol", [P, NGAIN])
    ssq = sb("ssq", [P, 10, 2, 4])
    stat = sb("stat", [P, 10, 4, 2])
    nmx = sb("nmx", [P, 2])
    rsum = sb("rsum", [P, 2])
    rinv = sb("rinv", [P, 2])

    s1 = ExitStack()
    gates = sb("gates", [P, 2, 4096], c=s1)
    qkv = sb("qkv", [P, 2, 3072], c=s1)
    cacc = sb("cacc", [P, 8, T], c=s1)
    oh = sb("oh", [P, 8, T], F32R, c=s1)
    ol = sb("ol", [P, 8, T], F32R, c=s1)
    bias = sb("bias", [P, 2, T], c=s1)
    bflip = sb("bflip", [P, 2, T], c=s1)
    stage1 = sb("stage1", [P, 2, 2, DH], c=s1)
    qkt1 = sb("qkt1", [P, 2, T], c=s1)
    prob1 = sb("prob1", [P, 2, T], c=s1)
    pt1 = sb("pt1", [P, 2, T], c=s1)
    ost1 = sb("ost1", [P, 2, DH], c=s1)
    wdw = sb("wdw", [P, 8, 32], c=s1)
    maskna = sb("maskna", [P, 64], c=s1)
    s1a = ExitStack()
    csq = sb("csq", [P, 8, T], c=s1a)
    s1a.close()
    cl = sb("cl", [P, 8, T], F32R, c=s1)
    s1b = ExitStack()
    zt = sb("zt", [P, 8, T + 2 * PAD], c=s1b)
    s1b.close()
    ch = sb("ch", [P, 8, T], F32R, c=s1)
    s1.close()
    s0 = ExitStack()
    xin = sb("xin", [P, 2, D], c=s0)
    gload = sb("gload", [P, P], c=s0)
    dwload = sb("dwload", [32, D_CONV], c=s0)
    rload = sb("rload", [P, 32], c=s0)
    rpad = sb("rpad", [P, P], c=s0)
    s0.close()

    hres = sb("hres", [P, 2, D])
    gpost = sb("gpost", [P, D])
    s2 = ExitStack()
    fh = sb("fh", [P, 44, T], F32R, c=s2)
    fl = sb("fl", [P, 44, T], F32R, c=s2)
    s2.close()
    s3 = ExitStack()
    aqkv = sb("aqkv", [P, 2, 3072], c=s3)
    uq = sb("uq", [P, 2, 1536], c=s3)
    ukv = sb("ukv", [P, 2, 2048], c=s3)
    lh = sb("lh", [P, 8, T], F32R, c=s3)
    ll = sb("ll", [P, 8, T], F32R, c=s3)
    kr = sb("kr", [P, 2, ROPE_B], c=s3)
    krt = sb("krt", [ROPE_B, T], c=s3)
    qrt = sb("qrt", [ROPE_B, T], c=s3)
    masks = sb("masks", [P, 2, 2, T], c=s3)
    stage2 = sb("stage2", [P, 2, 2, DH], c=s3)
    stager = sb("stager", [P, 2, ROPE_B], c=s3)
    qkt2 = sb("qkt2", [P, 2, T], c=s3)
    s3a = ExitStack()
    rtmp = sb("rtmp", [P, 4, 256], c=s3a)
    s3a.close()
    prob2 = sb("prob2", [P, 2, T], c=s3)
    pt2 = sb("pt2", [P, 2, T], c=s3)
    ost2 = sb("ost2", [P, 2, DH], c=s3)
    ang = sb("ang", [P, 5, 2, 48], c=s3)
    posi = sb("posi", [P, 2], I32, c=s3)
    posf = sb("posf", [P, 2], c=s3)
    invf = sb("invf", [P, 48], c=s3)
    s3.close()
    s4 = ExitStack()
    uh = sb("uh", [P, 32, T], F32R, c=s4)
    ul = sb("ul", [P, 32, T], F32R, c=s4)
    acc = sb("acc", [P, 2, D], c=s4)
    s4.close()

    psA = ctx.enter_context(nc.psum_tensor("psA", [P, 2, N], F32))
    psB = ctx.enter_context(nc.psum_tensor("psB", [P, 2, N], F32))
    psT = ctx.enter_context(nc.psum_tensor("psT", [P, 2, N], F32))
    ps6 = ctx.enter_context(nc.psum_tensor("ps6", [P, N], F32))
    ps7 = ctx.enter_context(nc.psum_tensor("ps7", [P, N], F32))

    raw_in = [sem(f"raw_in{i}") for i in range(4)]
    hi_ready = sem("hi_ready")
    lo_ready = sem("lo_ready")
    used = sem("used")
    a_free = sem("a_free")
    b_free = sem("b_free")
    tsrc = sem("tsrc")
    tdone = sem("tdone")
    thi = sem("thi")
    tlo = sem("tlo")
    x_in = sem("x_in")
    id_in = sem("id_in")
    gl_in = sem("gl_in")
    dw_in = sem("dw_in")
    rp_in = sem("rp_in")
    mk_in = sem("mk_in")
    rp_out = sem("rp_out")
    bias_in = sem("bias_in")
    hres_in = sem("hres_in")
    gp_in = sem("gp_in")
    c2_in = sem("c2_in")
    zeroed = sem("zeroed")
    cols_t = sem("cols_t")
    cols_e = sem("cols_e")
    acs = sem("acs")
    var_ok = sem("var_ok")
    sq_ok = sem("sq_ok")
    rs_ok = sem("rs_ok")
    mrg = sem("mrg")
    tap = sem("tap")
    mu_ok = sem("mu_ok")
    xc_ok = sem("xc_ok")
    csq_ok = sem("csq_ok")
    cv_ok = sem("cv_ok")
    cvv = sem("cvv")
    cvs = sem("cvs")
    xn_ok = sem("xn_ok")
    sil_ok = sem("sil_ok")
    ch_ok = sem("ch_ok")
    cl_ok = sem("cl_ok")
    bias_ok = sem("bias_ok")
    staged = sem("staged")
    qk_t = sem("qk_t")
    qk_e = sem("qk_e")
    sc_ok = sem("sc_ok")
    sm_ok = sem("sm_ok")
    mx_ok = sem("mx_ok")
    ex_ok = sem("ex_ok")
    p_t = sem("p_t")
    p_e = sem("p_e")
    pv_ok = sem("pv_ok")
    ri_ok = sem("ri_ok")
    o_ok = sem("o_ok")
    o_t = sem("o_t")
    o_hi = sem("o_hi")
    o_lo = sem("o_lo")
    kr_ok = sem("kr_ok")
    kr_e = sem("kr_e")
    kr_t = sem("kr_t")
    krt_ok = sem("krt_ok")
    tab = sem("tab")
    ang_ok = sem("ang_ok")
    sin_ok = sem("sin_ok")
    rot = sem("rot")
    out_in = sem("out_in")
    vec = sem("vec")
    acc_ok = sem("acc_ok")

    rpb_tab = nc.dram_tensor("rpb_padded", (120, 128), F32).ap()

    def wview(w):
        return w.rearrange("(c k p) n -> c p k n", k=2, p=P)

    w_in, w_ao, w_co, w_out = (wview(a[n][0]) for n in ("w_in", "w_attn_o", "w_conv_o", "w_out"))
    w_gu, w_dn, w_in2 = (wview(a[n][0]) for n in ("w_gate_up", "w_down", "w_in_2"))
    w_uq, w_ukv, w_out2 = (wview(a[n][0]) for n in ("w_uq_2", "w_ukv_2", "w_out_2"))
    w_up2, w_dn2 = (wview(a[n][0]) for n in ("w_up_2", "w_down_2"))
    w_kr = a["w_in_2"][0].rearrange("(k p) n -> p k n", p=P)[:, :, 4096:4096 + ROPE_B]
    x_v = a["x"][0].rearrange("(m p) d -> p m d", p=P)
    out_v = out[0].rearrange("(m p) d -> p m d", p=P)

    block = ctx.enter_context(nc.Block())

    def flat(v):
        return v.rearrange("p a b -> p (a b)")

    def backwards(v):
        step, count = v.ap[-1]
        return bass.AP(v.tensor, v.offset + step * (count - 1), [list(d) for d in v.ap[:-1]] + [[-step, count]])

    def raw_value(b, per, it):
        return 16 * (b // 4 + 1) + 4 * per * it

    @block.sync
    def _(sp):
        sp.dma_start(xin[:], x_v).then_inc(x_in, 16)
        sp.dma_start(ident[:], a["ident"]).then_inc(id_in, 16)

        def load(b, per, i, src):
            if not isinstance(i, int) or b + per * i >= 4:
                sp.wait_ge(lo_ready, i * per + (b - 3))
            sp.dma_start(raw[:, b % 4, :].rearrange("p (k n) -> p k n", k=2), src).then_inc(raw_in[b % 4], 16)

        def pair(name, per, i, wa, ca, wb, cb, step, k0=0, perm=None):
            b = C0[name] - per
            for half, (w, c) in enumerate(((wa, ca), (wb, cb))):
                for k in range(per // 2):
                    load(b + half * per // 2 + k, per, i,
                         w[k0 + (perm[k] if perm else k), :, :, bass.ds(i * step + (c - step), N) if step else slice(c, c + N)])

        for j in range(2):
            b = C0["conv_in"] + 16 * j
            for i in range(2):
                for k in range(8):
                    load(b + 8 * i + k, 0, 0, w_in[k, :, :, 3072 + 1024 * i + N * j:3072 + 1024 * i + N * j + N])
        with sp.Fori(1, 4) as i:
            pair("qkv", 16, i, w_in, 0, w_in, N, 1024)
        with sp.Fori(1, 5) as i:
            pair("gates", 16, i, w_in, 5120, w_in, 5120 + N, 1024)
        with sp.Fori(1, 5) as i:
            pair("merge", 8, i, w_ao, 0, w_co, 0, N)
        with sp.Fori(1, 3) as i:
            pair("out1", 16, i, w_out, 0, w_out, N, 1024)
        with sp.Fori(1, 12) as i:
            pair("ff1", 16, i, w_gu, 0, w_gu, D_FF, N, perm=PERM)
        with sp.Fori(1, 3) as i:
            pair("down1", 44, i, w_dn, 0, w_dn, N, 1024)
        pair("latent", 16, 1, w_in2, 3072, w_in2, 3584, 0, perm=PERM)
        sp.wait_ge(lo_ready, C0["krope"] - 3)
        sp.dma_start(raw[:, C0["krope"] % 4, :].rearrange("p (k n) -> p k n", k=16), w_kr)\
            .then_inc(raw_in[C0["krope"] % 4], 16)
        with sp.Fori(1, 4) as i:
            pair("aqkv", 16, i, w_in2, 0, w_in2, N, 1024, perm=PERM)
        for i in range(7):
            w, c = (w_uq, N * i) if i < 3 else (w_ukv, N * (i - 3))
            for k in range(2):
                load(C0["up_lat"] + 2 * i + k, 0, 0, w[k, :, :, c:c + N])
        with sp.Fori(1, 3) as i:
            pair("out2", 16, i, w_out2, 0, w_out2, N, 1024)
        for half, (up, dn) in enumerate((("up2a", "down2a"), ("up2b", "down2b"))):
            with sp.Fori(1, 5) as i:
                pair(up, 16, i, w_up2, 4096 * half, w_up2, 4096 * half + N, 1024, perm=PERM)
            with sp.Fori(1, 3) as i:
                pair(dn, 32, i, w_dn2, 0, w_dn2, N, 1024, k0=16 * half)

        for g in range(4):
            sp.wait_ge(tsrc, G0["end"] - 3 + g)
            sp.dma_start(out_v[:, :, N * g:N * g + N], hres[:, :, N * g:N * g + N]).then_inc(out_in, 16)
        sp.wait_ge(out_in, 64)

    @block.gpsimd
    def _(pool):
        nc.gpsimd.memset(rpad[:], 0.0).then_inc(zeroed, 1)
        nc.gpsimd.memset(dwload[:], 0.0).then_inc(zeroed, 1)
        nc.gpsimd.memset(zt[:], 0.0).then_inc(zeroed, 1)
        nc.gpsimd.memset(ones[:], 1.0 / D_CONV).then_inc(zeroed, 1)
        col = 0
        for name, n in GAINS:
            pool.dma_start(gload[col:col + n, :], a[name][0].rearrange("(k p) -> k p", p=P)).then_inc(gl_in, 16)
            col += n
        pool.wait_ge(zeroed, 2)
        pool.dma_start(dwload[0:TAPS, :], a["w_dw"][0]).then_inc(dw_in, 16)
        pool.dma_start(maskna[:], a["mask_na"]).then_inc(mk_in, 16)
        pool.dma_start(rload[0:120, 0:31], a["rpb"][0].rearrange("h r c -> (h r) c")).then_inc(rp_in, 16)
        pool.wait_ge(rp_in, 16)
        pool.wait_ge(zeroed, 1)
        nc.gpsimd.tensor_copy(rpad[0:120, 48:79], backwards(rload[0:120, 0:31])).then_inc(zeroed, 1)
        pool.wait_ge(zeroed, 5)
        pool.dma_start(rpb_tab, rpad[0:120, :]).then_inc(rp_out, 16)
        pool.wait_ge(rp_out, 16)
        pool.wait_ge(mk_in, 16)
        maskq = maskna[:, 0:64].unsqueeze(1).to_broadcast([P, 8, 64])

        def head_bias(h):
            for r in range(4):
                src = bass.AP(rpb_tab.tensor, (15 * h + 7 - r) * 128, [[1, 64], [128, 4], [1, 64]])
                dst = bflip[64 * (r % 2):64 * (r % 2) + 64, r // 2, :].rearrange("p (i c) -> p i c", i=4)
                pool.dma_start(dst, src).then_inc(bias_in, 16)
            pool.wait_ge(bias_in, 64 * (h + 1))
            if h >= 1:
                pool.wait_ge(sm_ok, h)
            nc.gpsimd.tensor_tensor(bias[:].rearrange("p m (i c) -> p (m i) c", c=64),
                                    backwards(bflip[:].rearrange("p m (i c) -> p (m i) c", c=64)),
                                    maskq, ALU.add).then_inc(bias_ok, 1)
            pool.wait_ge(bias_ok, h + 1)

        for h in range(H):
            head_bias(h)
            if h == 0:
                pool.wait_ge(a_free, A0["gates"])
                pool.wait_ge(b_free, B0["gates"])
            if h >= 1:
                pool.wait_ge(qk_t, h)
            for i in range(2):
                cp = nc.gpsimd.tensor_copy(stage1[:, i, :, :], qkv[:, :, 1024 * i + DH * h:1024 * i + DH * h + DH])
            cp.then_inc(staged, 1)

        pool.wait_ge(tsrc, G0["h1"] - 4)
        pool.dma_start(hres[:], x_v).then_inc(hres_in, 16)
        pool.dma_start(gpost[:], a["mix_post_g"].partition_broadcast(P)).then_inc(gp_in, 16)
        pool.wait_ge(tsrc, G0["f"] - 4)
        pool.dma_start(gpost[:], a["ffn_post_g"].partition_broadcast(P)).then_inc(gp_in, 16)
        pool.wait_ge(tsrc, G0["latent"] - 4)
        pool.dma_start(gpost[:], a["norm_attn_post_2"].partition_broadcast(P)).then_inc(gp_in, 16)
        pool.dma_start(masks[:, 0, :, :], a["log_count"].rearrange("(m p) k -> p m k", p=P)).then_inc(c2_in, 16)
        pool.dma_start(masks[:, 1, :, :], a["causal"].rearrange("(m p) k -> p m k", p=P)).then_inc(c2_in, 16)
        pool.dma_start(posi[:], a["positions_2"][0].rearrange("(m p) -> p m", p=P), allow_slow_non_contiguous=True).then_inc(c2_in, 16)
        pool.dma_start(invf[:], a["inv_freq"].partition_broadcast(P)).then_inc(c2_in, 16)

        def rope(x1, x2, f0, heads, r, step):
            n = heads * r
            for m in range(2):
                cos = ang[:, 0, m, f0:f0 + r].unsqueeze(1).to_broadcast([P, heads, r])
                sin = ang[:, 1, m, f0:f0 + r].unsqueeze(1).to_broadcast([P, heads, r])
                t = [rtmp[:, i, 0:n].rearrange("p (h r) -> p h r", r=r) for i in range(4)]
                if step[0]:
                    pool.wait_ge(rot, step[0])
                nc.gpsimd.tensor_tensor(t[0], x1[:, m], cos, ALU.mult)
                nc.gpsimd.tensor_tensor(t[1], x2[:, m], sin, ALU.mult)
                nc.gpsimd.tensor_tensor(t[2], x2[:, m], cos, ALU.mult)
                nc.gpsimd.tensor_tensor(t[3], x1[:, m], sin, ALU.mult).then_inc(rot, 1)
                pool.wait_ge(rot, step[0] + 1)
                nc.gpsimd.tensor_tensor(x1[:, m], t[0], t[1], ALU.subtract)
                nc.gpsimd.tensor_tensor(x2[:, m], t[2], t[3], ALU.add).then_inc(rot, 1)
                step[0] += 2

        def heads_view(buf, c0, width, lo_, r):
            return buf[:, :, c0:c0 + H * width].rearrange("p m (h w) -> p m h w", w=width)[:, :, :, lo_:lo_ + r]

        step = [0]
        pool.wait_ge(sin_ok, 2)
        pool.wait_ge(kr_e, 1)
        rope(kr[:, :, 0:32].unsqueeze(2), kr[:, :, 32:64].unsqueeze(2), 0, 1, 32, step)
        pool.wait_ge(a_free, A0["aqkv"] + 2)
        pool.wait_ge(b_free, B0["aqkv"] + 2)
        for i in range(2):
            rope(heads_view(aqkv, 1024 * i, DH, 0, 16), heads_view(aqkv, 1024 * i, DH, 16, 16), 32, H, 16, step)
        pool.wait_ge(a_free, A0["up_lat"] + 2)
        pool.wait_ge(b_free, B0["up_lat"] + 1)
        rope(heads_view(uq, 0, 192, 128, 32), heads_view(uq, 0, 192, 160, 32), 0, H, 32, step)
        pool.wait_ge(rot, step[0])
        with pool.Fori(0, 8) as it:
            pool.wait_ge(qk_t, it + 8)
            nc.gpsimd.tensor_copy(stage2[:, 0, :, :], aqkv[:, :, bass.ds(it * DH, DH)])
            nc.gpsimd.tensor_copy(stage2[:, 1, :, :], aqkv[:, :, bass.ds(it * DH + 1024, DH)]).then_inc(staged, 1)
        pool.wait_ge(a_free, A0["out2"])
        pool.wait_ge(b_free, B0["out2"])
        with pool.Fori(0, 8) as it:
            pool.wait_ge(qk_t, it + 16)
            nc.gpsimd.tensor_copy(stager[:], uq[:, :, bass.ds(it * 192 + 128, ROPE_B)])
            nc.gpsimd.tensor_copy(stage2[:, 0, :, :], uq[:, :, bass.ds(it * 192, DH)])
            nc.gpsimd.tensor_copy(stage2[:, 1, :, :], ukv[:, :, bass.ds(it * 256, DH)]).then_inc(staged, 1)
        pool.wait_ge(tsrc, G0["u0"] - 4)
        pool.dma_start(gpost[:], a["norm_mlp_post_2"].partition_broadcast(P)).then_inc(gp_in, 16)

    @block.scalar
    def _(act):
        def split(b, per=0, it=0):
            if b >= TOTAL:
                return
            act.wait_ge(raw_in[b % 4], raw_value(b, per, it))
            if b >= 4:
                act.wait_ge(used, b + per * it - 3)
            nc.scalar.activation(hi[:, b % 4, :], raw[:, b % 4, :], ACT.Copy).then_inc(hi_ready, 1)

        sums = [0]

        def square(src, dst, k):
            if sums[0] >= 2:
                act.wait_ge(acs, sums[0] - 1)
            nc.scalar.activation(dst, src, ACT.Square, accum_out=k).then_inc(acs, 1)
            sums[0] += 1

        def group_hi(g, dst, gain=None, when=None):
            act.wait_ge(tdone, g + 1 if when is None else when)
            if gain is None:
                nc.scalar.activation(flat(dst), flat(psT[:]), ACT.Copy).then_inc(thi, 1)
                return
            for j in range(4):
                ins = nc.scalar.activation(dst[:, j, :], psT[:, j // 2, T * (j % 2):T * (j % 2) + T], ACT.Copy,
                                           scale=gcol[:, gain + j:gain + j + 1])
            ins.then_inc(thi, 1)

        roots = [0]

        def root(k):
            act.wait_ge(var_ok, roots[0] + 1)
            nc.scalar.activation(stat[:, k, 1, :], stat[:, k, 0, :], ACT.Sqrt).then_inc(sq_ok, 1)
            roots[0] += 1

        def rstd(k, m):
            return stat[:, k, 3, m:m + 1]

        for c in range(AHEAD):
            split(c)
        act.wait_ge(x_in, 16)
        for m in range(2):
            for q in range(4):
                square(xin[:, m, N * q:N * q + N], sg[:, q % 2, :], ssq[:, 0, m, q:q + 1])
        act.wait_ge(cols_e, 1)
        for g in range(4):
            group_hi(g, xh[:, 4 * g:4 * g + 4, :], GC["mix_pre_g"] + 4 * g)
        root(0)

        for j in range(2):
            b = C0["conv_in"] + 16 * j
            for c in range(16):
                if j == 1 and c == 1:
                    act.wait_ge(zeroed, 3)
                    act.wait_ge(tdone, G0["z"] + 1)
                    nc.scalar.activation(zt[:, 0:2, PAD:PAD + T], psT[:, 0, :].rearrange("p (a t) -> p a t", a=2),
                                         ACT.Copy).then_inc(thi, 1)
                if c == 15:
                    act.wait_ge(used, b + 16)
                    if j == 0:
                        act.wait_ge(rs_ok, 1)
                        act.wait_ge(acs, SUMS["x"])
                    else:
                        act.wait_ge(tsrc, 1)
                    for m in range(2):
                        ins = nc.scalar.activation(sg[:, m, :], psB[:, m, :], ACT.Sigmoid, scale=rstd(0, m))
                    ins.then_inc(b_free, 1)
                split(b + c + AHEAD)

        def qkv_pair(it, first):
            b = C0["qkv"]
            for c in range(16):
                if first and c == 1:
                    act.wait_ge(tdone, G0["z"] + 2)
                    nc.scalar.activation(zt[:, 4:6, PAD:PAD + T], psT[:, 0, :].rearrange("p (a t) -> p a t", a=2),
                                         ACT.Copy).then_inc(thi, 1)
                for half, ps, free in ((0, psA, a_free), (1, psB, b_free)):
                    if c == 7 + 8 * half:
                        act.wait_ge(used, b + 16 * it + c + 1)
                        for m in range(2):
                            ins = nc.scalar.activation(qkv[:, m, bass.ds(it * 1024 + N * half, N)], ps[:, m, :],
                                                       ACT.Copy, scale=rstd(0, m))
                        ins.then_inc(free, 1)
                split(b + c + AHEAD, 16, it)

        qkv_pair(0, True)
        with act.Fori(1, 3) as it:
            qkv_pair(it, False)

        def qk_out(n, dst, busy):
            act.wait_ge(qk_t, n + 1)
            if busy is not None:
                act.wait_ge(sc_ok, busy)
            return nc.scalar.activation(flat(dst[:]), ps6[:], ACT.Copy)

        def exps(n, prob):
            act.wait_ge(mx_ok, n + 1)
            for m in range(2):
                ins = nc.scalar.activation(prob[:, m, :], prob[:, m, :], ACT.Exp, bias=nmx[:, m:m + 1],
                                           accum_out=rsum[:, m:m + 1])
            ins.then_inc(ex_ok, 1)

        def p_out(n, pt, busy):
            act.wait_ge(p_t, n + 1)
            if busy is not None:
                act.wait_ge(pv_ok, busy)
            nc.scalar.activation(flat(pt[:]), ps6[:], ACT.Copy).then_inc(p_e, 1)

        def o_high(n, dst):
            act.wait_ge(o_t, n + 1)
            nc.scalar.activation(dst, ps6[:, 0:T], ACT.Copy).then_inc(o_hi, 1)

        for j in range(4):
            b = C0["gates"] + 16 * j
            for c in range(16):
                n, s = 2 * j + c // 8, c % 8
                if s == 0:
                    qk_out(n, qkt1, n if n else None).then_inc(qk_e, 1)
                if s == 3 and n:
                    o_high(n - 1, oh[:, n - 1, :])
                if s == 4:
                    exps(n, prob1)
                if s == 6:
                    p_out(n, pt1, n if n else None)
                if s == 7:
                    ps, free = (psA, a_free) if c < 8 else (psB, b_free)
                    act.wait_ge(used, b + c + 1)
                    for m in range(2):
                        ins = nc.scalar.activation(gates[:, m, 1024 * j + 64 * (c - 7):1024 * j + 64 * (c - 7) + N],
                                                   ps[:, m, :], ACT.Sigmoid, scale=rstd(0, m))
                    ins.then_inc(free, 1)
                if j == 2 and c == 2:
                    act.wait_ge(xc_ok, 1)
                    nc.scalar.activation(csq[:], cacc[:], ACT.Square).then_inc(csq_ok, 1)
                if j == 2 and c == 8:
                    act.wait_ge(cvv, 1)
                    nc.scalar.activation(st[:, 0, 1, 0:T], st[:, 0, 0, 0:T], ACT.Sqrt).then_inc(cvs, 1)
                if j == 2 and c == 13:
                    act.wait_ge(xn_ok, 1)
                    for t in range(8):
                        ins = nc.scalar.activation(cacc[:, t, :], cacc[:, t, :], ACT.Silu,
                                                   bias=gcol[:, GC["conv_ln_b"] + t:GC["conv_ln_b"] + t + 1],
                                                   scale=gcol[:, GC["conv_ln_g"] + t:GC["conv_ln_g"] + t + 1])
                    ins.then_inc(sil_ok, 1)
                if j == 3 and c == 1:
                    act.wait_ge(sil_ok, 1)
                    nc.scalar.activation(ch[:], cacc[:], ACT.Copy).then_inc(ch_ok, 1)
                split(b + c + AHEAD)
        o_high(7, oh[:, 7, :])

        def merge_pair(it, first):
            b = C0["merge"]
            for c in range(8):
                if not first and c == 1:
                    group_hi(0, xh[:, bass.ds(it * 4 - 4, 4), :], when=it + G0["merged"])
                split(b + c + AHEAD, 8, it)

        merge_pair(0, True)
        with act.Fori(1, 4) as it:
            merge_pair(it, False)

        def normed_pairs(name, per, k, before=None):
            for j in range(2):
                b = C0[name] + per * j
                for c in range(per):
                    if before is not None and j == 0 and c == 1:
                        before()
                    for half, ps in ((0, psA), (1, psB)):
                        if c == per // 2 - 1 + half * per // 2:
                            act.wait_ge(used, b + c + 1)
                            for m in range(2):
                                square(ps[:, m, :], sg[:, m, :], ssq[:, k, m, 2 * j + half:2 * j + half + 1])
                    if j < 1 or c < per - 1:
                        split(b + c + AHEAD)
            root(k)

        def post(name, per, k, g0, gain):
            for i, q in enumerate(ORDER):
                group_hi(g0 + i, xh[:, 4 * q:4 * q + 4, :], gain + 4 * q)
                if i == 0:
                    split(C0[name] + 2 * per - 1 + AHEAD)
                else:
                    split(C0[name] + 2 * per + 2 * i - 2 + AHEAD)
                    split(C0[name] + 2 * per + 2 * i - 1 + AHEAD)
            for q in range(4):
                for m in range(2):
                    square(hres[:, m, N * q:N * q + N], sg[:, m, :], ssq[:, k, m, q:q + 1])
            root(k)

        normed_pairs("out1", 16, 1, lambda: group_hi(9, xh[:, 12:16, :]))
        post("out1", 16, 2, G0["h1"], GC["ffn_pre_g"])

        def ff1_pair(it, first):
            b = C0["ff1"]
            for c in range(6 if first else 0, 16):
                if not first and c == 1:
                    group_hi(0, fh[:, bass.ds(it * 4 - 4, 4), :], when=it + G0["f"])
                if c == 7:
                    act.wait_ge(used, b + 16 * it + 8)
                    if not first:
                        act.wait_ge(tsrc, it + G0["f"] - 4)
                    else:
                        act.wait_ge(acs, SUMS["h1"])
                        act.wait_ge(rs_ok, 3)
                    for m in range(2):
                        ins = nc.scalar.activation(sg[:, m, :], psA[:, m, :], ACT.Silu, scale=rstd(2, m))
                    ins.then_inc(a_free, 1)
                split(b + c + AHEAD, 16, it)

        ff1_pair(0, True)
        with act.Fori(1, 11) as it:
            ff1_pair(it, False)

        normed_pairs("down1", 44, 3, lambda: group_hi(24, fh[:, 40:44, :]))
        post("down1", 44, 4, G0["h2"], GC["norm_attn_pre_2"])

        b = C0["latent"]
        for c in range(6, 16):
            split(b + c + AHEAD)
        act.wait_ge(ang_ok, 1)
        nc.scalar.activation(ang[:, 1, :, :], ang[:, 3, :, :], ACT.Sin).then_inc(sin_ok, 1)
        nc.scalar.activation(ang[:, 0, :, :], ang[:, 4, :, :], ACT.Sin).then_inc(sin_ok, 1)
        split(C0["krope"] + AHEAD)

        def aqkv_pair(it, first):
            b = C0["aqkv"]
            for c in range(16):
                if first and c == 1:
                    act.wait_ge(tsrc, G0["h3"] - 4)
                    for k in range(2):
                        for m in range(2):
                            square(st[:, k, m, :], sg[:, m, :], ssq[:, 5 + k, m, 0:1])
                    group_hi(29, lh[:, 0:4, :], GC["q_latent_norm_2"])
                if first and c == 3:
                    group_hi(30, lh[:, 4:8, :], GC["kv_latent_norm_2"])
                    root(5)
                    root(6)
                for half, ps, free in ((0, psA, a_free), (1, psB, b_free)):
                    if c == 7 + 8 * half:
                        act.wait_ge(used, b + 16 * it + c + 1)
                        if first:
                            act.wait_ge(rs_ok, 5)
                        for m in range(2):
                            ins = nc.scalar.activation(aqkv[:, m, bass.ds(it * 1024 + N * half, N)], ps[:, m, :],
                                                       ACT.Copy, scale=rstd(4, m))
                        ins.then_inc(free, 1)
                split(b + c + AHEAD, 16, it)

        aqkv_pair(0, True)
        with act.Fori(1, 3) as it:
            aqkv_pair(it, False)
        for i in range(7):
            ps, free = (psA, a_free) if i % 2 == 0 else (psB, b_free)
            dst, c, k = (uq, N * i, 5) if i < 3 else (ukv, N * (i - 3), 6)
            split(C0["up_lat"] + 2 * i + AHEAD)
            act.wait_ge(used, C0["up_lat"] + 2 * i + 2)
            act.wait_ge(rs_ok, 7)
            for m in range(2):
                ins = nc.scalar.activation(dst[:, m, c:c + N], ps[:, m, :], ACT.Copy, scale=rstd(k, m))
            ins.then_inc(free, 1)
            split(C0["up_lat"] + 2 * i + 1 + AHEAD)

        act.wait_ge(kr_t, 1)
        nc.scalar.activation(krt[:], psT[0:ROPE_B, 0, 0:T], ACT.Copy).then_inc(krt_ok, 1)
        with act.Fori(0, 8) as it:
            n = it + 8
            qk_out(n, qkt2, n).then_inc(qk_e, 1)
            exps(n, prob2)
            p_out(n, pt2, n)
            o_high(n, xh[:, bass.ds(it, 1), :].rearrange("p a t -> p (a t)"))
        with act.Fori(0, 8) as it:
            n = it + 16
            qk_out(n, qkt2, n)
            nc.scalar.activation(qrt[:], psT[0:ROPE_B, 0, 0:T], ACT.Copy).then_inc(qk_e, 1)
            exps(n, prob2)
            p_out(n, pt2, n)
            o_high(n, xh[:, bass.ds(it + 8, 1), :].rearrange("p a t -> p (a t)"))

        normed_pairs("out2", 16, 7)
        post("out2", 16, 8, G0["h3"], GC["norm_mlp_pre_2"])

        def up_pair(name, it, first, g0, start):
            b = C0[name]
            for c in range(start if first else 0, 16):
                if not first and c == 1:
                    group_hi(0, uh[:, bass.ds(it * 8 - 4, 4), :], when=it * 2 + g0)
                if c == 9:
                    group_hi(0, uh[:, bass.ds(it * 8, 4), :], when=it * 2 + g0 + 1)
                for half, ps, free in ((0, psA, a_free), (1, psB, b_free)):
                    if c == 7 + 8 * half:
                        act.wait_ge(used, b + 16 * it + c + 1)
                        act.wait_ge(tdone, it * 2 + g0 + half - 1)
                        if first:
                            act.wait_ge(rs_ok, 9)
                        for m in range(2):
                            ins = nc.scalar.activation(st[:, half, m, :], ps[:, m, :], ACT.Relu, scale=rstd(8, m))
                        ins.then_inc(free, 1)
                split(b + c + AHEAD, 16, it)

        def down_pairs(name, g_last):
            for j in range(2):
                for c in range(32):
                    if j == 0 and c == 1:
                        group_hi(g_last, uh[:, 28:32, :])
                    split(C0[name] + 32 * j + c + AHEAD)

        up_pair("up2a", 0, True, G0["u0"], 6)
        with act.Fori(1, 4) as it:
            up_pair("up2a", it, False, G0["u0"], 0)
        down_pairs("down2a", G0["u0"] + 7)
        up_pair("up2b", 0, True, G0["u1"], 0)
        with act.Fori(1, 4) as it:
            up_pair("up2b", it, False, G0["u1"], 0)
        down_pairs("down2b", G0["u1"] + 7)
        act.wait_ge(acc_ok, 4)
        for q in range(4):
            for m in range(2):
                square(acc[:, m, N * q:N * q + N], sg[:, m, :], ssq[:, 9, m, q:q + 1])
        root(9)

    @block.vector
    def _(v):
        chain = [0]

        def link(ins):
            chain[0] += 1
            ins.then_inc(vec, 1)
            v.wait_ge(vec, chain[0])

        def split(b, per=0, it=0):
            if b >= TOTAL:
                return
            v.wait_ge(hi_ready, b + per * it + 1)
            nc.vector.tensor_tensor(lo[:, b % 4, :], raw[:, b % 4, :], hi[:, b % 4, :].bitcast(F32),
                                    ALU.subtract).then_inc(lo_ready, 1)

        def group_lo(g, dst_l, dst_h, gain=None, when=None):
            v.wait_ge(thi, g + 1 if when is None else when)
            if gain is None:
                nc.vector.tensor_tensor(flat(dst_l), flat(psT[:]), flat(dst_h).bitcast(F32),
                                        ALU.subtract).then_inc(tlo, 1)
                return
            for j in range(4):
                ins = nc.vector.scalar_tensor_tensor(
                    out=dst_l[:, j, :], in0=psT[:, j // 2, T * (j % 2):T * (j % 2) + T],
                    scalar=gcol[:, gain + j:gain + j + 1], in1=dst_h[:, j, :].bitcast(F32),
                    op0=ALU.mult, op1=ALU.subtract)
            ins.then_inc(tlo, 1)

        roots = [0]

        def variance(k, width, parts, need):
            v.wait_ge(acs, need)
            link(nc.vector.tensor_reduce(stat[:, k, 1, :], ssq[:, k, :, 0:parts], AX_X, ALU.add))
            nc.vector.tensor_scalar(stat[:, k, 0, :], stat[:, k, 1, :], 1.0 / width, EPS, ALU.mult,
                                    ALU.add).then_inc(var_ok, 1)

        def inverse_root(var, root_, y, t, dst):
            link(nc.vector.reciprocal(y, root_))
            link(nc.vector.tensor_tensor(t, y, y, ALU.mult))
            link(nc.vector.tensor_tensor(t, t, var, ALU.mult))
            link(nc.vector.tensor_scalar(t, t, -0.5, 1.5, ALU.mult, ALU.add))
            return nc.vector.tensor_tensor(dst, y, t, ALU.mult)

        def finish(k):
            v.wait_ge(sq_ok, roots[0] + 1)
            roots[0] += 1
            inverse_root(stat[:, k, 0, :], stat[:, k, 1, :], stat[:, k, 2, :], stat[:, k, 1, :],
                         stat[:, k, 3, :]).then_inc(rs_ok, 1)
            v.wait_ge(rs_ok, roots[0])

        def rstd(k, m):
            return stat[:, k, 3, m:m + 1]

        v.wait_ge(cols_t, 1)
        nc.vector.tensor_copy(gcol[:], ps7[:, 0:NGAIN])
        nc.vector.tensor_copy(flat(wdw[:]), ps6[:, 0:256]).then_inc(cols_e, 1)
        v.wait_ge(cols_e, 1)
        for c in range(AHEAD):
            split(c)
        for g in range(4):
            group_lo(g, xl[:, 4 * g:4 * g + 4, :], xh[:, 4 * g:4 * g + 4, :], GC["mix_pre_g"] + 4 * g)
        variance(0, D, 4, SUMS["x"])
        finish(0)

        def z_out(g, t):
            v.wait_ge(thi, g + 1)
            v.wait_ge(zeroed, 3)
            nc.vector.tensor_copy(zt[:, t:t + 2, PAD:PAD + T],
                                  psT[:, 1, :].rearrange("p (a t) -> p a t", a=2)).then_inc(tlo, 1)

        for j in range(2):
            b = C0["conv_in"] + 16 * j
            for c in range(16):
                if j == 1 and c == 1:
                    z_out(G0["z"], 2)
                if c == 15:
                    v.wait_ge(used, b + 16)
                    v.wait_ge(b_free, B0["conv_in"] + j + 1)
                    for m in range(2):
                        ins = nc.vector.scalar_tensor_tensor(out=st[:, j, m, :], in0=psA[:, m, :],
                                                             scalar=rstd(0, m), in1=sg[:, m, :],
                                                             op0=ALU.mult, op1=ALU.mult)
                    ins.then_inc(tsrc, 1)
                split(b + c + AHEAD)

        def conv_tap(ct, count, i):
            z = zt[:, bass.ds(ct, 1), i:i + T].rearrange("p a t -> p (a t)")
            acc_ = cacc[:, bass.ds(ct, 1), :].rearrange("p a t -> p (a t)")
            w = wdw[:, bass.ds(ct, 1), i:i + 1].rearrange("p a t -> p (a t)")
            if i == 0:
                bdw = gcol[:, bass.ds(ct + GC["b_dw"], 1)]
                nc.vector.tensor_scalar(acc_, z, w, bdw, ALU.mult, ALU.add).then_inc(tap, 1)
                return
            v.wait_ge(tap, count)
            nc.vector.scalar_tensor_tensor(out=acc_, in0=z, scalar=w, in1=acc_, op0=ALU.mult,
                                           op1=ALU.add).then_inc(tap, 1)

        def qkv_pair(it, first):
            for c in range(16):
                if first and c == 1:
                    z_out(G0["z"] + 1, 6)
                if first and c == 2:
                    v.wait_ge(tlo, G0["z"] + 2)
                for i in range(4 * c, min(4 * c + 4, 2 * TAPS)):
                    conv_tap(it * 2 + i // TAPS, it * (2 * TAPS) + i, i % TAPS)
                split(C0["qkv"] + c + AHEAD, 16, it)

        qkv_pair(0, True)
        with v.Fori(1, 3) as it:
            qkv_pair(it, False)

        def softmax(n, prob, scale, bias_, first=False):
            v.wait_ge(sc_ok, n + 1)
            if not first:
                v.wait_ge(p_t, n)
            nc.vector.scalar_tensor_tensor(out=flat(prob[:]), in0=ps7[:], scalar=scale, in1=bias_,
                                           op0=ALU.mult, op1=ALU.add).then_inc(sm_ok, 1)
            v.wait_ge(sm_ok, n + 1)
            nc.vector.tensor_reduce(nmx[:], prob[:], AX_X, ALU.max, negate=True).then_inc(mx_ok, 1)

        def o_out(n, ost, first=False):
            v.wait_ge(pv_ok, n + 1)
            if not first:
                v.wait_ge(o_t, n)
            nc.vector.reciprocal(rinv[:], rsum[:]).then_inc(ri_ok, 1)
            v.wait_ge(ri_ok, n + 1)
            for m in range(2):
                ins = nc.vector.tensor_scalar(ost[:, m, :], ps7[:, DH * m:DH * m + DH], rinv[:, m:m + 1],
                                              None, ALU.mult)
            ins.then_inc(o_ok, 1)

        def o_low(n, dst_l, dst_h):
            v.wait_ge(o_hi, n + 1)
            nc.vector.tensor_tensor(dst_l, ps6[:, 0:T], dst_h.bitcast(F32), ALU.subtract).then_inc(o_lo, 1)

        cv, cs_, cy, ct_ = (st[:, i // 2, i % 2, 0:T] for i in range(4))
        for j in range(4):
            for c in range(16):
                n, s = 2 * j + c // 8, c % 8
                if s == 2:
                    v.wait_ge(bias_ok, n + 1)
                    softmax(n, prob1, SCALE_A, flat(bias[:]), first=(n == 0))
                if s == 3 and n:
                    o_low(n - 1, ol[:, n - 1, :], oh[:, n - 1, :])
                if s == 7:
                    o_out(n, ost1, first=(n == 0))
                if j < 2:
                    for i in range(2 * c, min(2 * c + 2, TAPS)):
                        conv_tap(6 + j, (6 + j) * TAPS + i, i)
                if j == 2 and c == 1:
                    v.wait_ge(mu_ok, 1)
                    v.wait_ge(tap, 8 * TAPS)
                    nc.vector.tensor_tensor(cacc[:], cacc[:], psT[:, 0, 0:T].unsqueeze(1).to_broadcast([P, 8, T]),
                                            ALU.subtract).then_inc(xc_ok, 1)
                if j == 2 and c == 7:
                    v.wait_ge(cv_ok, 1)
                    nc.vector.tensor_scalar(cv, psT[:, 1, 0:T], EPS, None, ALU.add).then_inc(cvv, 1)
                if j == 2 and c == 9:
                    v.wait_ge(cvs, 1)
                    link(inverse_root(cv, cs_, cy, ct_, cs_))
                if j == 2 and c == 11:
                    v.wait_ge(csq_ok, 1)
                    nc.vector.tensor_tensor(cacc[:], cacc[:], cs_.unsqueeze(1).to_broadcast([P, 8, T]),
                                            ALU.mult).then_inc(xn_ok, 1)
                if j == 3 and c == 3:
                    v.wait_ge(ch_ok, 1)
                    nc.vector.tensor_tensor(cl[:], cacc[:], ch[:].bitcast(F32), ALU.subtract).then_inc(cl_ok, 1)
                split(C0["gates"] + 16 * j + c + AHEAD)
        o_low(7, ol[:, 7, :], oh[:, 7, :])

        def merge_pair(it, first):
            b = C0["merge"]
            for c in range(8):
                if not first and c == 1:
                    group_lo(0, xl[:, bass.ds(it * 4 - 4, 4), :], xh[:, bass.ds(it * 4 - 4, 4), :],
                             when=it + G0["merged"])
                if c == 3:
                    v.wait_ge(used, b + 8 * it + 4)
                    for m in range(2):
                        ins = nc.vector.tensor_tensor(sg[:, m, :], psA[:, m, :], gates[:, m, bass.ds(it * N, N)],
                                                      ALU.mult)
                    ins.then_inc(a_free, 1)
                if c == 7:
                    v.wait_ge(used, b + 8 * it + 8)
                    if not first:
                        v.wait_ge(tdone, it + G0["merged"])
                    v.wait_ge(a_free, it + A0["merge"] + 1)
                    for m in range(2):
                        ins = nc.vector.tensor_tensor(st[:, 0, m, :], psB[:, m, :],
                                                      gates[:, m, bass.ds(it * N + D, N)], ALU.mult)
                    ins.then_inc(mrg, 1)
                    v.wait_ge(mrg, it + 1)
                    nc.vector.tensor_tensor(st[:, 0, :, :], st[:, 0, :, :], sg[:], ALU.add).then_inc(tsrc, 1)
                split(b + c + AHEAD, 8, it)

        merge_pair(0, True)
        with v.Fori(1, 4) as it:
            merge_pair(it, False)

        def normed_pairs(name, per, k, gains_in, last_group=None):
            need = SUMS[name] - 8
            for j in range(2):
                b = C0[name] + per * j
                for c in range(per):
                    if j == 0 and c == 1 and last_group is not None:
                        last_group()
                    for half, ps, free in ((0, psA, a_free), (1, psB, b_free)):
                        if j == 0 and c == per // 2 - 1 + half * per // 2:
                            v.wait_ge(acs, need + 2 * half + 2)
                            if half == 0:
                                v.wait_ge(gp_in, gains_in)
                            for m in range(2):
                                ins = nc.vector.tensor_tensor(st[:, half, m, :], ps[:, m, :],
                                                              gpost[:, N * half:N * half + N], ALU.mult)
                            ins.then_inc(free, 1)
                    if j < 1 or c < per - 1:
                        split(b + c + AHEAD)
            variance(k, D, 4, SUMS[name])
            finish(k)

        def post(name, per, k, k_next, g0, gain, sums):
            def low(i):
                q = ORDER[i]
                group_lo(g0 + i, xl[:, 4 * q:4 * q + 4, :], xh[:, 4 * q:4 * q + 4, :], gain + 4 * q)

            for i, q in enumerate(ORDER):
                if q >= 2:
                    ps = psA if q == 2 else psB
                    if i:
                        v.wait_ge(tsrc, g0 + i - 4)
                    for m in range(2):
                        ins = nc.vector.scalar_tensor_tensor(out=sg[:, m, :], in0=ps[:, m, :], scalar=rstd(k, m),
                                                             in1=gpost[:, N * q:N * q + N], op0=ALU.mult,
                                                             op1=ALU.mult)
                    link(ins)
                    nc.vector.tensor_tensor(hres[:, :, N * q:N * q + N], hres[:, :, N * q:N * q + N], sg[:],
                                            ALU.add).then_inc(tsrc, 1)
                else:
                    for m in range(2):
                        ins = nc.vector.scalar_tensor_tensor(out=hres[:, m, N * q:N * q + N], in0=st[:, q, m, :],
                                                             scalar=rstd(k, m), in1=hres[:, m, N * q:N * q + N],
                                                             op0=ALU.mult, op1=ALU.add)
                    ins.then_inc(tsrc, 1)
                if i == 0:
                    split(C0[name] + 2 * per - 1 + AHEAD)
                else:
                    low(i - 1)
                if i >= 2:
                    split(C0[name] + 2 * per + 2 * i - 4 + AHEAD)
                    split(C0[name] + 2 * per + 2 * i - 3 + AHEAD)
            low(3)
            split(C0[name] + 2 * per + 4 + AHEAD)
            split(C0[name] + 2 * per + 5 + AHEAD)
            variance(k_next, D, 4, sums)
            finish(k_next)

        normed_pairs("out1", 16, 1, 16, lambda: group_lo(9, xl[:, 12:16, :], xh[:, 12:16, :]))
        v.wait_ge(hres_in, 16)
        post("out1", 16, 1, 2, G0["h1"], GC["ffn_pre_g"], SUMS["h1"])

        def ff1_pair(it, first):
            b = C0["ff1"]
            for c in range(6 if first else 0, 16):
                if not first and c == 1:
                    group_lo(0, fl[:, bass.ds(it * 4 - 4, 4), :], fh[:, bass.ds(it * 4 - 4, 4), :],
                             when=it + G0["f"])
                if c == 15:
                    v.wait_ge(used, b + 16 * it + 16)
                    v.wait_ge(a_free, it + A0["ff1"] + 1)
                    if not first:
                        v.wait_ge(tdone, it + G0["f"])
                    for m in range(2):
                        ins = nc.vector.scalar_tensor_tensor(out=st[:, 0, m, :], in0=psB[:, m, :],
                                                             scalar=rstd(2, m), in1=sg[:, m, :],
                                                             op0=ALU.mult, op1=ALU.mult)
                    ins.then_inc(tsrc, 1)
                split(b + c + AHEAD, 16, it)

        ff1_pair(0, True)
        with v.Fori(1, 11) as it:
            ff1_pair(it, False)

        normed_pairs("down1", 44, 3, 32, lambda: group_lo(24, fl[:, 40:44, :], fh[:, 40:44, :]))
        post("down1", 44, 3, 4, G0["h2"], GC["norm_attn_pre_2"], SUMS["h2"])

        def angles():
            v.wait_ge(c2_in, 64)
            link(nc.vector.tensor_copy(posf[:], posi[:]))
            for m in range(2):
                ins = nc.vector.tensor_scalar(ang[:, 2, m, :], invf[:], posf[:, m:m + 1], None, ALU.mult)
            link(ins)
            big = 12582912.0
            turns, r, rc = flat(ang[:, 3, :, :]), flat(ang[:, 2, :, :]), flat(ang[:, 4, :, :])
            link(nc.vector.tensor_scalar(turns, r, 1.0 / TWO_PI, big, ALU.mult, ALU.add))
            link(nc.vector.tensor_scalar(turns, turns, -big, None, ALU.add))
            p1, p2 = 6.28125, 0.0019340515136718750
            p3 = TWO_PI - p1 - p2
            for part in (p1, p2, p3):
                link(nc.vector.scalar_tensor_tensor(out=r, in0=turns, scalar=-part, in1=r, op0=ALU.mult,
                                                    op1=ALU.add))
            link(nc.vector.tensor_scalar(turns, r, PI_LO, -PI_LO, ALU.min, ALU.max))
            link(nc.vector.tensor_scalar(rc, r, TWO_PI / 4, None, ALU.add))
            link(nc.vector.tensor_scalar(r, rc, TWO_PI / 2, -TWO_PI, ALU.is_gt, ALU.mult))
            link(nc.vector.tensor_tensor(rc, rc, r, ALU.add))
            nc.vector.tensor_scalar(rc, rc, PI_LO, -PI_LO, ALU.min, ALU.max).then_inc(ang_ok, 1)

        for c in range(6, 16):
            for half, ps in ((0, psA), (1, psB)):
                if c == 7 + 8 * half:
                    v.wait_ge(used, C0["latent"] + c + 1)
                    for m in range(2):
                        ins = nc.vector.tensor_scalar(st[:, half, m, :], ps[:, m, :], rstd(4, m), None, ALU.mult)
                    ins.then_inc(tsrc, 1)
            if c == 9:
                angles()
            split(C0["latent"] + c + AHEAD)
        v.wait_ge(used, C0["krope"] + 1)
        for m in range(2):
            ins = nc.vector.tensor_scalar(kr[:, m, :], ps6[:, ROPE_B * m:ROPE_B * m + ROPE_B], rstd(4, m), None,
                                          ALU.mult)
        ins.then_inc(kr_e, 1)
        split(C0["krope"] + AHEAD)

        def aqkv_pair(it, first):
            for c in range(16):
                if first and c == 1:
                    group_lo(29, ll[:, 0:4, :], lh[:, 0:4, :], GC["q_latent_norm_2"])
                if first and c == 3:
                    group_lo(30, ll[:, 4:8, :], lh[:, 4:8, :], GC["kv_latent_norm_2"])
                    variance(5, RANK, 1, SUMS["latent"])
                    variance(6, RANK, 1, SUMS["latent"])
                    finish(5)
                    finish(6)
                split(C0["aqkv"] + c + AHEAD, 16, it)

        aqkv_pair(0, True)
        with v.Fori(1, 3) as it:
            aqkv_pair(it, False)
        for c in range(14):
            split(C0["up_lat"] + c + AHEAD)

        with v.Fori(0, 8) as it:
            n = it + 8
            softmax(n, prob2, SCALE_A, flat(masks[:, 0, :, :]))
            o_out(n, ost2)
            o_low(n, xl[:, bass.ds(it, 1), :].rearrange("p a t -> p (a t)"),
                  xh[:, bass.ds(it, 1), :].rearrange("p a t -> p (a t)"))
        with v.Fori(0, 8) as it:
            n = it + 16
            softmax(n, prob2, SCALE_B, flat(masks[:, 1, :, :]))
            o_out(n, ost2)
            o_low(n, xl[:, bass.ds(it + 8, 1), :].rearrange("p a t -> p (a t)"),
                  xh[:, bass.ds(it + 8, 1), :].rearrange("p a t -> p (a t)"))

        normed_pairs("out2", 16, 7, 48)
        post("out2", 16, 7, 8, G0["h3"], GC["norm_mlp_pre_2"], SUMS["h3"])

        def up_pair(name, it, first, g0, start):
            b = C0[name]
            for c in range(start if first else 0, 16):
                if not first and c == 1:
                    group_lo(0, ul[:, bass.ds(it * 8 - 4, 4), :], uh[:, bass.ds(it * 8 - 4, 4), :],
                             when=it * 2 + g0)
                if c == 9:
                    group_lo(0, ul[:, bass.ds(it * 8, 4), :], uh[:, bass.ds(it * 8, 4), :], when=it * 2 + g0 + 1)
                for half, free, f0 in ((0, a_free, A0[name]), (1, b_free, B0[name])):
                    if c == 7 + 8 * half:
                        v.wait_ge(free, it + f0 + 1)
                        nc.vector.tensor_tensor(st[:, half, :, :], st[:, half, :, :], st[:, half, :, :],
                                                ALU.mult).then_inc(tsrc, 1)
                split(b + c + AHEAD, 16, it)

        def down_pairs(name, g_last, add):
            for j in range(2):
                b = C0[name] + 32 * j
                for c in range(32):
                    if j == 0 and c == 1:
                        group_lo(g_last, ul[:, 28:32, :], uh[:, 28:32, :])
                    for half, ps, free in ((0, psA, a_free), (1, psB, b_free)):
                        if c == 15 + 16 * half:
                            v.wait_ge(used, b + c + 1)
                            dst = acc[:, :, N * (2 * j + half):N * (2 * j + half) + N]
                            if add:
                                nc.vector.tensor_tensor(dst, dst, ps[:], ALU.add).then_inc(acc_ok, 1)
                            else:
                                nc.vector.tensor_copy(dst, ps[:]).then_inc(free, 1)
                    split(b + c + AHEAD)

        up_pair("up2a", 0, True, G0["u0"], 6)
        with v.Fori(1, 4) as it:
            up_pair("up2a", it, False, G0["u0"], 0)
        down_pairs("down2a", G0["u0"] + 7, False)
        up_pair("up2b", 0, True, G0["u1"], 0)
        with v.Fori(1, 4) as it:
            up_pair("up2b", it, False, G0["u1"], 0)
        down_pairs("down2b", G0["u1"] + 7, True)
        variance(9, D, 4, SUMS["down2"])
        finish(9)
        v.wait_ge(gp_in, 64)
        for q in range(4):
            for m in range(2):
                part = acc[:, m, N * q:N * q + N]
                ins = nc.vector.scalar_tensor_tensor(out=part, in0=part, scalar=rstd(9, m),
                                                     in1=gpost[:, N * q:N * q + N], op0=ALU.mult, op1=ALU.mult)
            link(ins)
            nc.vector.tensor_tensor(hres[:, :, N * q:N * q + N], hres[:, :, N * q:N * q + N],
                                    acc[:, :, N * q:N * q + N], ALU.add).then_inc(tsrc, 1)

    @block.tensor
    def _(pe):
        def chunk(out_, x_h, x_l, kts, first, last, b, per=0, it=0):
            pe.wait_ge(lo_ready, b + per * it + 1)
            for i, k in enumerate(kts):
                w_h, w_l = hi[:, b % 4, N * i:N * i + N], lo[:, b % 4, N * i:N * i + N]
                for m in range(2):
                    s_h, s_l = x_h[:, k, P * m:P * m + P], x_l[:, k, P * m:P * m + P]
                    nc.tensor.matmul(out_[:, m, :], s_h, w_h, start=(first and i == 0), stop=False)
                    nc.tensor.matmul(out_[:, m, :], s_h, w_l, start=False, stop=False)
                    ins = nc.tensor.matmul(out_[:, m, :], s_l, w_h, start=False, stop=(last and i == 1))
            ins.then_inc(used, 1)

        def group_t(g, src, when=None):
            if not (isinstance(g, int) and g == 0):
                pe.wait_ge(tlo, g)
            if when is not None:
                pe.wait_ge(tsrc, when)
            for j in range(4):
                for m in range(2):
                    ins = nc.tensor.transpose(psT[:, j // 2, T * (j % 2) + P * m:T * (j % 2) + P * m + P],
                                              src[:, m, P * j:P * j + P], ident[:])
            ins.then_inc(tdone, 1)

        def pair(name, per, it, x_h, x_l, a_wait, b_wait, hook=None, perm=None, k0=0, start=None):
            half = per // 2
            for c in range(per):
                if start is not None:
                    start(c)
                for first, ps, wait in ((0, psA, a_wait), (half, psB, b_wait)):
                    if c == first and wait is not None:
                        pe.wait_ge(*wait)
                k = c % half
                kk = 2 * (perm[k] if perm else k)
                chunk(psB if c >= half else psA, x_h, x_l, (kk, kk + 1), k == 0, k == half - 1, C0[name] + c,
                      per, it)
                if hook is not None:
                    hook(c)

        pe.wait_ge(id_in, 16)
        pe.wait_ge(gl_in, 16 * len(GAINS))
        nc.tensor.transpose(ps7[:, 0:NGAIN], gload[0:NGAIN, :], ident[0:NGAIN, 0:NGAIN])
        pe.wait_ge(dw_in, 16)
        for t in range(8):
            ins = nc.tensor.transpose(ps6[:, 32 * t:32 * t + 32], dwload[:, P * t:P * t + P], ident[0:32, 0:32])
        ins.then_inc(cols_t, 1)
        pe.wait_ge(x_in, 16)
        for g in range(4):
            group_t(g, xin[:, :, N * g:N * g + N])
        pe.wait_ge(tlo, 4)

        def z_hook(g):
            return lambda c: group_t(g, st[:, g - G0["z"], :, :], when=g - 3) if c == 1 else None

        pair("conv_in", 16, 0, xh, xl, None, None)
        def pair_at(off, *args, **kw):
            C0["_"] = off
            pair("_", *args, **kw)

        pair_at(C0["conv_in"] + 16, 16, 0, xh, xl, (tsrc, 1), (b_free, 1), z_hook(4))
        pair("qkv", 16, 0, xh, xl, (tsrc, 2), (b_free, B0["qkv"]), z_hook(5))
        with pe.Fori(1, 3) as it:
            pair("qkv", 16, it, xh, xl, (a_free, it + A0["qkv"]), (b_free, it + B0["qkv"]))

        def qk_turn(n, stage, first=False):
            pe.wait_ge(staged, n + 1)
            if not first:
                pe.wait_ge(p_e, n)
            for i in range(2):
                for m in range(2):
                    ins = nc.tensor.transpose(ps6[:, T * i + P * m:T * i + P * m + P], stage[:, i, m, :], ident[:])
            return ins

        def scores(n, qkt, first=False, rope_=False):
            pe.wait_ge(qk_e, n + 1)
            if not first:
                pe.wait_ge(o_ok, n)
            for m in range(2):
                ins = nc.tensor.matmul(ps7[:, T * m:T * m + T], qkt[:, 0, P * m:P * m + P], qkt[:, 1, :],
                                       start=True, stop=not rope_)
                if rope_:
                    ins = nc.tensor.matmul(ps7[:, T * m:T * m + T], qrt[:, P * m:P * m + P], krt[:],
                                           start=False, stop=True)
            ins.then_inc(sc_ok, 1)

        def p_turn(n, prob, bank6):
            pe.wait_ge(ex_ok, n + 1)
            if bank6 is not None:
                pe.wait_ge(*bank6)
            for k in range(2):
                for m in range(2):
                    ins = nc.tensor.transpose(ps6[:, T * k + P * m:T * k + P * m + P], prob[:, m, P * k:P * k + P],
                                              ident[:])
            ins.then_inc(p_t, 1)

        def values(n, pt, v_of):
            pe.wait_ge(p_e, n + 1)
            for m in range(2):
                for k in range(2):
                    ins = nc.tensor.matmul(ps7[:, DH * m:DH * m + DH], pt[:, k, P * m:P * m + P], v_of(k),
                                           start=(k == 0), stop=(k == 1))
            ins.then_inc(pv_ok, 1)

        def o_turn(n, ost, bank6):
            pe.wait_ge(o_ok, n + 1)
            pe.wait_ge(*bank6)
            for m in range(2):
                ins = nc.tensor.transpose(ps6[:, P * m:P * m + P], ost[:, m, :], ident[:])
            ins.then_inc(o_t, 1)

        for j in range(4):
            def hook(c, j=j):
                n, s = 2 * j + c // 8, c % 8
                if s == 0:
                    qk_turn(n, stage1, first=(n == 0)).then_inc(qk_t, 1)
                if s == 2:
                    scores(n, qkt1, first=(n == 0))
                if s == 3 and n:
                    o_turn(n - 1, ost1, (qk_e, n + 1))
                if s == 5:
                    p_turn(n, prob1, (o_lo, n) if n else None)
                if s == 7:
                    values(n, pt1, lambda k: qkv[:, k, 2048 + DH * n:2048 + DH * n + DH])
                if j == 2 and c == 0:
                    pe.wait_ge(tap, 8 * TAPS)
                    pe.wait_ge(tlo, G0["merged"])
                    pe.wait_ge(zeroed, 4)
                    for t in range(8):
                        ins = nc.tensor.matmul(psT[:, 0, 0:T], ones[:], cacc[:, t, :], start=(t == 0),
                                               stop=(t == 7))
                    ins.then_inc(mu_ok, 1)
                if j == 2 and c == 5:
                    pe.wait_ge(csq_ok, 1)
                    for t in range(8):
                        ins = nc.tensor.matmul(psT[:, 1, 0:T], ones[:], csq[:, t, :], start=(t == 0),
                                               stop=(t == 7))
                    ins.then_inc(cv_ok, 1)

            pair_at(C0["gates"] + 16 * j, 16, 0, xh, xl, (a_free, A0["gates"] + j), (b_free, B0["gates"] + j), hook)
        o_turn(7, ost1, (p_e, 8))
        pe.wait_ge(o_lo, 8)
        pe.wait_ge(cl_ok, 1)

        def merge_pair(it, first):
            for c in range(8):
                if c == 0:
                    pe.wait_ge(a_free, it + A0["merge"])
                if c == 4 and first:
                    pe.wait_ge(b_free, B0["merge"])
                x_h, x_l, ps = (oh, ol, psA) if c < 4 else (ch, cl, psB)
                chunk(ps, x_h, x_l, (2 * (c % 4), 2 * (c % 4) + 1), c % 4 == 0, c % 4 == 3, C0["merge"] + c, 8, it)
                if c == 1 and not first:
                    group_t(it + (G0["merged"] - 1), st[:, 0, :, :], when=it + (G0["merged"] - 4))

        merge_pair(0, True)
        with pe.Fori(1, 4) as it:
            merge_pair(it, False)

        def need_last(g, c0):
            return lambda c: pe.wait_ge(tlo, g + 1) if c == c0 else None

        def post(g0):
            group_t(g0, hres[:, :, N * ORDER[0]:N * ORDER[0] + N], when=g0 - 3)

            def start(c):
                if c % 2 == 0 and c // 2 < 4:
                    i = c // 2
                    pe.wait_ge(tlo, g0 + i + 1)
                    if i < 3:
                        q = ORDER[i + 1]
                        group_t(g0 + i + 1, hres[:, :, N * q:N * q + N], when=g0 + i + 1 - 3)
            return start

        pair("out1", 16, 0, xh, xl, (a_free, A0["out1"]), None,
             lambda c: group_t(9, st[:, 0, :, :], when=6) if c == 1 else None, start=need_last(9, 6))
        pair_at(C0["out1"] + 16, 16, 0, xh, xl, (a_free, A0["out1"] + 1), (b_free, B0["out1"] + 1))

        pair("ff1", 16, 0, xh, xl, None, None, perm=PERM, start=post(G0["h1"]))
        with pe.Fori(1, 11) as it:
            pair("ff1", 16, it, xh, xl, (a_free, it + A0["ff1"]), None,
                 lambda c: group_t(it + (G0["f"] - 1), st[:, 0, :, :], when=it + (G0["f"] - 4)) if c == 1 else None,
                 perm=PERM)

        pair("down1", 44, 0, fh, fl, (a_free, A0["down1"]), None,
             lambda c: group_t(24, st[:, 0, :, :], when=21) if c == 1 else None, start=need_last(24, 20))
        pair_at(C0["down1"] + 44, 44, 0, fh, fl, (a_free, A0["down1"] + 1), (b_free, B0["down1"] + 1))

        pair("latent", 16, 0, xh, xl, None, None, perm=PERM, start=post(G0["h2"]))
        pe.wait_ge(lo_ready, C0["krope"] + 1)
        pe.wait_ge(o_lo, 8)
        s = C0["krope"] % 4
        for m in range(2):
            for k in range(16):
                w_h, w_l = hi[:, s, ROPE_B * k:ROPE_B * k + ROPE_B], lo[:, s, ROPE_B * k:ROPE_B * k + ROPE_B]
                dst = ps6[:, ROPE_B * m:ROPE_B * m + ROPE_B]
                nc.tensor.matmul(dst, xh[:, k, P * m:P * m + P], w_h, start=(k == 0), stop=False)
                nc.tensor.matmul(dst, xh[:, k, P * m:P * m + P], w_l, start=False, stop=False)
                ins = nc.tensor.matmul(dst, xl[:, k, P * m:P * m + P], w_h, start=False, stop=(k == 15))
        ins.then_inc(used, 1)

        def lat_hook(c):
            if c in (1, 3):
                i = c // 2
                group_t(G0["latent"] + i, st[:, i, :, :], when=G0["latent"] + i - 3)

        pair("aqkv", 16, 0, xh, xl, (tsrc, 26), (tsrc, 27), lat_hook, perm=PERM)
        with pe.Fori(1, 3) as it:
            pair("aqkv", 16, it, xh, xl, (a_free, it + A0["aqkv"]), (b_free, it + B0["aqkv"]), perm=PERM)
        pe.wait_ge(tlo, G0["latent"] + 2)
        for i in range(7):
            ps, free, f0 = (psA, a_free, A0["up_lat"]) if i % 2 == 0 else (psB, b_free, B0["up_lat"])
            pe.wait_ge(free, f0 + i // 2)
            k0 = 0 if i < 3 else 4
            for c in range(2):
                chunk(ps, lh, ll, (k0 + 2 * c, k0 + 2 * c + 1), c == 0, c == 1, C0["up_lat"] + 2 * i + c)

        pe.wait_ge(rot, 4)
        for m in range(2):
            ins = nc.tensor.transpose(psT[0:ROPE_B, 0, P * m:P * m + P], kr[:, m, :], ident[:])
        ins.then_inc(kr_t, 1)
        pe.wait_ge(krt_ok, 1)
        pe.wait_ge(kr_e, 1)
        pe.wait_ge(a_free, A0["aqkv"] + 3)
        with pe.Fori(0, 8) as it:
            n = it + 8
            qk_turn(n, stage2).then_inc(qk_t, 1)
            scores(n, qkt2)
            p_turn(n, prob2, None)
            values(n, pt2, lambda k: aqkv[:, k, bass.ds(it * DH + 2048, DH)])
            o_turn(n, ost2, (p_e, n + 1))
            pe.wait_ge(o_lo, n + 1)
        with pe.Fori(0, 8) as it:
            n = it + 16
            qk_turn(n, stage2)
            for m in range(2):
                ins = nc.tensor.transpose(psT[0:ROPE_B, 0, P * m:P * m + P], stager[:, m, :], ident[:])
            ins.then_inc(qk_t, 1)
            scores(n, qkt2, rope_=True)
            p_turn(n, prob2, None)
            values(n, pt2, lambda k: ukv[:, k, bass.ds(it * 256 + DH, DH)])
            o_turn(n, ost2, (p_e, n + 1))
            pe.wait_ge(o_lo, n + 1)

        for j in range(2):
            pair_at(C0["out2"] + 16 * j, 16, 0, xh, xl, (a_free, A0["out2"] + j), (b_free, B0["out2"] + j))

        for half, (up, dn, u) in enumerate((("up2a", "down2a", "u0"), ("up2b", "down2b", "u1"))):
            def up_hook(it, first):
                def hook(c):
                    if c == 1 and not first:
                        group_t(it * 2 + (G0[u] - 1), st[:, 1, :, :], when=it * 2 + (G0[u] - 4))
                    if c == 9:
                        group_t(it * 2 + G0[u], st[:, 0, :, :], when=it * 2 + (G0[u] - 3))
                return hook

            waits = (None, None) if half == 0 else ((a_free, A0[up]), (b_free, B0[up]))
            pair(up, 16, 0, xh, xl, *waits, up_hook(0, True), perm=PERM, start=post(G0["h3"]) if half == 0 else None)
            with pe.Fori(1, 4) as it:
                pair(up, 16, it, xh, xl, (a_free, it + A0[up]), (b_free, it + B0[up]), up_hook(it, False), perm=PERM)
            g = G0[u] + 7
            pair(dn, 32, 0, uh, ul, (a_free, A0[dn]), (b_free, B0[dn]),
                 lambda c: group_t(g, st[:, 1, :, :], when=g - 3) if c == 1 else None, start=need_last(g, 14))
            pair_at(C0[dn] + 32, 32, 0, uh, ul,
                    (a_free, A0[dn] + 1) if half == 0 else (acc_ok, 1),
                    (b_free, B0[dn] + 1) if half == 0 else (acc_ok, 2))
    ctx.close()


def shape_constants():
    import numpy as np

    w, c = np.arange(64)[:, None], np.arange(64)[None, :]
    start = np.clip(w - 8, 0, 48)
    window = (c >= start) & (c < start + 16)
    q, k = np.arange(T)[:, None], np.arange(T)[None, :]
    causal = k <= q
    count = (causal & (q - k <= 128)).astype(int) + (causal & ((q - k) % 4 == 0)) + (causal & ((q - k) % 16 == 0))
    theta = 500000.0
    freq = [theta ** (-2.0 * i / ROPE_B) for i in range(32)] + [theta ** (-2.0 * i / ROPE_A) for i in range(16)]
    return {
        "ident": np.eye(P, dtype=np.float32),
        "mask_na": np.tile(np.where(window, 0.0, -1e30), (2, 1)).astype(np.float32),
        "log_count": np.where(count > 0, np.log(np.maximum(count, 1)), -1e30).astype(np.float32),
        "causal": np.where(causal, 0.0, -1e30).astype(np.float32),
        "inv_freq": np.asarray(freq, dtype=np.float32),
    }


def kernel(**inputs):
    import numpy as _np
    import concourse.bacc as _bacc
    from concourse import mybir as _mybir
    from concourse.bass_utils import run_bass_kernel_spmd as _run

    nc = _bacc.Bacc("TRN2", target_bir_lowering=False, num_devices=1)
    arrays, aps = {}, {}
    for name, array in {**inputs, **shape_constants()}.items():
        arr = _np.ascontiguousarray(array)
        if name in ("mix_post_g", "ffn_post_g", "norm_attn_post_2", "norm_mlp_post_2"):
            arr = arr.reshape(-1)
        arrays[f"in_{name}"] = arr
        aps[name] = nc.dram_tensor(f"in_{name}", arr.shape, _mybir.dt.from_np(arr.dtype), kind="ExternalInput").ap()
    out = nc.dram_tensor("out_0", (1, T, D), _mybir.dt.float32, kind="ExternalOutput").ap()
    build(nc, aps, out)
    r = _run(nc, [arrays], core_ids=[0])
    return r.results[0]["out_0"]
```

```python
from contextlib import ExitStack

import concourse.bass as bass
from concourse import mybir

F32 = mybir.dt.float32
F32R = mybir.dt.float32r
I32 = mybir.dt.int32
ACT = mybir.ActivationFunctionType
ALU = mybir.AluOpType
AX_X = mybir.AxisListType.X

P = 128
T = 256
D = 2048
H = 8
DH = 128
D_CONV = 1024
TAPS = 31
PAD = TAPS // 2
D_FF = 5632
D_FF2 = 8192
RANK = 512
ROPE_A = 32
ROPE_B = 64
EPS = 1e-6
N = 512
AHEAD = 4
SCALE_A = DH ** -0.5
SCALE_B = (DH + ROPE_B) ** -0.5

STAGES = [("conv_in", 2, 16), ("qkv", 3, 16), ("gates", 4, 16), ("merge", 4, 8), ("out1", 2, 16),
          ("ff1", 11, 16), ("down1", 2, 44), ("latent", 1, 16), ("krope", 1, 1), ("aq", 1, 16),
          ("up_lat", 7, 2), ("akv", 2, 16), ("out2", 2, 16), ("up2a", 4, 16), ("down2a", 2, 32), ("up2b", 4, 16),
          ("down2b", 2, 32)]
C0 = {}
TOTAL = 0
for _name, _pairs, _per in STAGES:
    C0[_name] = TOTAL
    TOTAL += _pairs * _per

A0, B0 = {}, {}
_a = _b = 0
for _name, _na, _nb in [("conv_in", 2, 0), ("qkv", 3, 3), ("gates", 4, 4), ("merge", 4, 0), ("out1", 1, 1),
                        ("ff1", 11, 0), ("down1", 1, 1), ("latent", 0, 0), ("aq", 1, 1), ("up_lat", 4, 3),
                        ("akv", 2, 2), ("out2", 2, 2), ("up2a", 4, 4), ("down2a", 2, 2), ("up2b", 4, 4), ("down2b", 2, 2)]:
    A0[_name], B0[_name] = _a, _b
    _a += _na
    _b += _nb

_sums = [("x", 8), ("out1", 8), ("h1", 8), ("down1", 8), ("h2", 8), ("latent", 4), ("out2", 8), ("h3", 8),
         ("down2", 8)]
SUMS = {n: sum(k for _, k in _sums[:i + 1]) for i, (n, _) in enumerate(_sums)}

ORDER = [2, 3, 0, 1]
PERM = [2 * q + i for q in ORDER for i in range(2)]

G0 = {"x": 0, "z": 4, "merged": 6, "h1": 10, "f": 14, "h2": 25, "latent": 29, "h3": 31, "u0": 35, "u1": 43,
      "end": 51}

HEADS2 = [(8 + i, 3 * i) for i in range(H)] + [(16 + i, 26 + 2 * i) for i in range(H)]
OUT2 = [(1, 0, 1), (1, 1, 1), (0, 0, 1), (0, 1, 1), (0, 0, 0), (0, 1, 0), (1, 0, 0), (1, 1, 0)]


def head_steps(slot, offset):
    return [n for n, first in HEADS2 if first + offset == slot]


GAINS = [("mix_pre_g", 16), ("ffn_pre_g", 16), ("norm_attn_pre_2", 16), ("norm_mlp_pre_2", 16),
         ("q_latent_norm_2", 4), ("kv_latent_norm_2", 4), ("conv_ln_g", 8), ("conv_ln_b", 8), ("b_dw", 8)]
GC = {}
_c = 0
for _name, _n in GAINS:
    GC[_name] = _c
    _c += _n
NGAIN = _c
FIRST = GAINS[0][1]

TWO_PI = 6.283185307179586
PI_LO = 3.1415925


def build(nc, a, out):
    ctx = ExitStack()

    def sb(name, shape, dt=F32, c=ctx):
        return c.enter_context(nc.sbuf_tensor(name, shape, dt))

    def sem(name):
        return ctx.enter_context(nc.semaphore(name))

    raw = sb("raw", [P, 4, 1024])
    hi = sb("hi", [P, 4, 1024], F32R)
    lo = sb("lo", [P, 4, 1024], F32R)
    xh = sb("xh", [P, 16, T], F32R)
    xl = sb("xl", [P, 16, T], F32R)
    st = sb("st", [P, 2, 2, N])
    sg = sb("sg", [P, 2, N])
    ident = sb("ident", [P, P])
    ones = sb("ones", [P, P])
    gcol = sb("gcol", [P, NGAIN])
    ssq = sb("ssq", [P, 10, 2, 4])
    stat = sb("stat", [P, 10, 4, 2])
    nmx = sb("nmx", [P, 2])
    rsum = sb("rsum", [P, 2, 2])
    rinv = sb("rinv", [P, 2])

    s1 = ExitStack()
    gates = sb("gates", [P, 2, 4096], c=s1)
    qkv = sb("qkv", [P, 2, 3072], c=s1)
    cacc = sb("cacc", [P, 8, T], c=s1)
    oh = sb("oh", [P, 8, T], F32R, c=s1)
    ol = sb("ol", [P, 8, T], F32R, c=s1)
    bias = sb("bias", [P, 2, T], c=s1)
    bflip = sb("bflip", [P, 2, T], c=s1)
    qkt1 = sb("qkt1", [P, 2, T], c=s1)
    prob1 = sb("prob1", [P, 2, T], c=s1)
    pt1 = sb("pt1", [P, 2, T], c=s1)
    ost1 = sb("ost1", [P, 2, DH], c=s1)
    wdw = sb("wdw", [P, 8, 32], c=s1)
    maskna = sb("maskna", [P, 64], c=s1)
    ptmp = sb("ptmp", [P, 2, T], c=s1)
    s1a = ExitStack()
    csq = sb("csq", [P, 8, T], c=s1a)
    s1a.close()
    cl = sb("cl", [P, 8, T], F32R, c=s1)
    s1b = ExitStack()
    zt = sb("zt", [P, 8, T + 2 * PAD], c=s1b)
    s1b.close()
    ch = sb("ch", [P, 8, T], F32R, c=s1)
    s1.close()
    s0 = ExitStack()
    xin = sb("xin", [P, 2, D], c=s0)
    gload = sb("gload", [P, P], c=s0)
    dwload = sb("dwload", [32, D_CONV], c=s0)
    rload = sb("rload", [P, 32], c=s0)
    rpad = sb("rpad", [P, P], c=s0)
    s0.close()

    hres = sb("hres", [P, 2, D])
    gpost = sb("gpost", [P, D])
    s2 = ExitStack()
    fh = sb("fh", [P, 44, T], F32R, c=s2)
    fl = sb("fl", [P, 44, T], F32R, c=s2)
    s2.close()
    s3 = ExitStack()
    aqkv = sb("aqkv", [P, 2, 3072], c=s3)
    uq = sb("uq", [P, 2, 1536], c=s3)
    ukv = sb("ukv", [P, 2, 2048], c=s3)
    lh = sb("lh", [P, 8, T], F32R, c=s3)
    ll = sb("ll", [P, 8, T], F32R, c=s3)
    kr = sb("kr", [P, 2, ROPE_B], c=s3)
    krt = sb("krt", [ROPE_B, T], c=s3)
    qrt = sb("qrt", [ROPE_B, T], c=s3)
    masks = sb("masks", [P, 2, 2, T], c=s3)
    qkt2 = sb("qkt2", [P, 2, T], c=s3)
    rtmp = sb("rtmp", [P, 4, 256], c=s3)
    prob2 = sb("prob2", [P, 2, T], c=s3)
    pt2 = sb("pt2", [P, 2, T], c=s3)
    ost2 = sb("ost2", [P, 2, DH], c=s3)
    ang = sb("ang", [P, 5, 2, 48], c=s3)
    posi = sb("posi", [P, 2], I32, c=s3)
    posf = sb("posf", [P, 2], c=s3)
    invf = sb("invf", [P, 48], c=s3)
    s3.close()
    s4 = ExitStack()
    uh = sb("uh", [P, 32, T], F32R, c=s4)
    ul = sb("ul", [P, 32, T], F32R, c=s4)
    acc = sb("acc", [P, 2, D], c=s4)
    s4.close()

    psA = ctx.enter_context(nc.psum_tensor("psA", [P, 2, N], F32))
    psB = ctx.enter_context(nc.psum_tensor("psB", [P, 2, N], F32))
    psT = ctx.enter_context(nc.psum_tensor("psT", [P, 2, N], F32))
    ps6 = ctx.enter_context(nc.psum_tensor("ps6", [P, N], F32))
    ps7 = ctx.enter_context(nc.psum_tensor("ps7", [P, N], F32))

    raw_in = [sem(f"raw_in{i}") for i in range(4)]
    hi_ready = sem("hi_ready")
    lo_ready = sem("lo_ready")
    used = sem("used")
    a_free = sem("a_free")
    b_free = sem("b_free")
    tsrc = sem("tsrc")
    tdone = sem("tdone")
    thi = sem("thi")
    tlo = sem("tlo")
    x_in = [sem(f"x_in{i}") for i in range(4)]
    id_in = sem("id_in")
    g1_in = sem("g1_in")
    gl_in = sem("gl_in")
    dw_in = sem("dw_in")
    rp_in = sem("rp_in")
    mk_in = sem("mk_in")
    rp_out = sem("rp_out")
    bias_in = sem("bias_in")
    hres_in = sem("hres_in")
    gp_in = sem("gp_in")
    c2_in = sem("c2_in")
    zeroed = sem("zeroed")
    cols_t = sem("cols_t")
    cols_e = sem("cols_e")
    acs = sem("acs")
    var_ok = sem("var_ok")
    sq_ok = sem("sq_ok")
    rs_ok = sem("rs_ok")
    mrg = sem("mrg")
    tap = sem("tap")
    ptap = sem("ptap")
    mu_ok = sem("mu_ok")
    xc_ok = sem("xc_ok")
    csq_ok = sem("csq_ok")
    cv_ok = sem("cv_ok")
    cvv = sem("cvv")
    cvs = sem("cvs")
    xn_ok = sem("xn_ok")
    sil_ok = sem("sil_ok")
    ch_ok = sem("ch_ok")
    cl_ok = sem("cl_ok")
    bias_ok = sem("bias_ok")
    qk_t = sem("qk_t")
    qk_e = sem("qk_e")
    sc_ok = sem("sc_ok")
    sm_ok = sem("sm_ok")
    mx_ok = sem("mx_ok")
    ex_ok = sem("ex_ok")
    p_t = sem("p_t")
    p_e = sem("p_e")
    pv_ok = sem("pv_ok")
    ri_ok = sem("ri_ok")
    o_ok = sem("o_ok")
    o_t = sem("o_t")
    o_hi = sem("o_hi")
    o_lo = sem("o_lo")
    kr_e = sem("kr_e")
    kr_t = sem("kr_t")
    krt_ok = sem("krt_ok")
    ang_ok = sem("ang_ok")
    sin_ok = sem("sin_ok")
    rot = sem("rot")
    out_in = sem("out_in")
    vec = sem("vec")
    acc_ok = sem("acc_ok")

    rpb_tab = nc.dram_tensor("rpb_padded", (120, 128), F32).ap()

    def wview(w):
        return w.rearrange("(c k p) n -> c p k n", k=2, p=P)

    w_in, w_ao, w_co, w_out = (wview(a[n][0]) for n in ("w_in", "w_attn_o", "w_conv_o", "w_out"))
    w_gu, w_dn, w_in2 = (wview(a[n][0]) for n in ("w_gate_up", "w_down", "w_in_2"))
    w_uq, w_ukv, w_out2 = (wview(a[n][0]) for n in ("w_uq_2", "w_ukv_2", "w_out_2"))
    w_up2, w_dn2 = (wview(a[n][0]) for n in ("w_up_2", "w_down_2"))
    w_kr = a["w_in_2"][0].rearrange("(k p) n -> p k n", p=P)[:, :, 4096:4096 + ROPE_B]
    x_v = a["x"][0].rearrange("(m p) d -> p m d", p=P)
    out_v = out[0].rearrange("(m p) d -> p m d", p=P)

    block = ctx.enter_context(nc.Block())

    def flat(v):
        return v.rearrange("p a b -> p (a b)")

    def backwards(v):
        step, count = v.ap[-1]
        return bass.AP(v.tensor, v.offset + step * (count - 1), [list(d) for d in v.ap[:-1]] + [[-step, count]])

    def raw_value(b, per, it):
        return 16 * (b // 4 + 1) + 4 * per * it

    @block.sync
    def _(sp):
        def load(b, per, i, src):
            if not isinstance(i, int) or b + per * i >= 4:
                sp.wait_ge(lo_ready, i * per + (b - 3))
            sp.dma_start(raw[:, b % 4, :].rearrange("p (k n) -> p k n", k=2), src).then_inc(raw_in[b % 4], 16)

        def pair(name, per, i, wa, ca, wb, cb, step, k0=0, perm=None):
            b = C0[name] - per
            for half, (w, c) in enumerate(((wa, ca), (wb, cb))):
                for k in range(per // 2):
                    load(b + half * per // 2 + k, per, i,
                         w[k0 + (perm[k] if perm else k), :, :, bass.ds(i * step + (c - step), N) if step else slice(c, c + N)])

        def load_x(q):
            sp.dma_start(xin[:, :, N * q:N * q + N], x_v[:, :, N * q:N * q + N]).then_inc(x_in[q], 16)

        load_x(0)
        sp.dma_start(ident[:], a["ident"]).then_inc(id_in, 16)
        for j in range(2):
            b = C0["conv_in"] + 16 * j
            for i in range(2):
                for k in range(8):
                    if j == 0 and i == 0 and k in (1, 2, 3):
                        load_x(k)
                    c = 3072 + 1024 * (1 - i) + N * j
                    load(b + 8 * i + k, 0, 0, w_in[k, :, :, c:c + N])
        with sp.Fori(1, 4) as i:
            pair("qkv", 16, i, w_in, 0, w_in, N, 1024)
        with sp.Fori(1, 5) as i:
            pair("gates", 16, i, w_in, 5120, w_in, 5120 + N, 1024)
        with sp.Fori(1, 5) as i:
            pair("merge", 8, i, w_ao, 0, w_co, 0, N)
        with sp.Fori(1, 3) as i:
            pair("out1", 16, i, w_out, 0, w_out, N, 1024)
        with sp.Fori(1, 12) as i:
            pair("ff1", 16, i, w_gu, 0, w_gu, D_FF, N, perm=PERM)
        with sp.Fori(1, 3) as i:
            pair("down1", 44, i, w_dn, 0, w_dn, N, 1024)
        pair("latent", 16, 1, w_in2, 3072, w_in2, 3584, 0, perm=PERM)
        sp.wait_ge(lo_ready, C0["krope"] - 3)
        sp.dma_start(raw[:, C0["krope"] % 4, :].rearrange("p (k n) -> p k n", k=16), w_kr)\
            .then_inc(raw_in[C0["krope"] % 4], 16)
        pair("aq", 16, 1, w_in2, 0, w_in2, N, 0, perm=PERM)
        for i in range(7):
            w, c = (w_uq, N * i) if i < 3 else (w_ukv, N * (i - 3))
            for k in range(2):
                load(C0["up_lat"] + 2 * i + k, 0, 0, w[k, :, :, c:c + N])
        for i in (1, 2):
            pair("akv", 16, i, w_in2, 1024, w_in2, 1024 + N, 1024, perm=PERM)
        for g, (j, bank, rows) in enumerate(OUT2):
            c = 1024 * j + N * bank
            for k in range(4):
                load(C0["out2"] + 4 * g + k, 0, 0, w_out2[4 * rows + k, :, :, c:c + N])
        for half, (up, dn) in enumerate((("up2a", "down2a"), ("up2b", "down2b"))):
            with sp.Fori(1, 5) as i:
                pair(up, 16, i, w_up2, 4096 * half, w_up2, 4096 * half + N, 1024, perm=PERM)
            with sp.Fori(1, 3) as i:
                pair(dn, 32, i, w_dn2, 0, w_dn2, N, 1024, k0=16 * half)

        for i, g in enumerate((3, 0, 1, 2)):
            sp.wait_ge(tsrc, G0["end"] - 3 + i)
            sp.dma_start(out_v[:, :, N * g:N * g + N], hres[:, :, N * g:N * g + N]).then_inc(out_in, 16)
        sp.wait_ge(out_in, 64)

    @block.gpsimd
    def _(pool):
        col = 0
        for name, n in GAINS:
            pool.dma_start(gload[col:col + n, :], a[name][0].rearrange("(k p) -> k p", p=P))\
                .then_inc(gl_in if col else g1_in, 16)
            col += n
        nc.gpsimd.memset(rpad[:], 0.0).then_inc(zeroed, 1)
        nc.gpsimd.memset(dwload[:], 0.0).then_inc(zeroed, 1)
        nc.gpsimd.memset(zt[:], 0.0).then_inc(zeroed, 1)
        nc.gpsimd.memset(ones[:], 1.0 / D_CONV).then_inc(zeroed, 1)
        pool.wait_ge(zeroed, 2)
        pool.dma_start(dwload[0:TAPS, :], a["w_dw"][0]).then_inc(dw_in, 16)
        pool.dma_start(maskna[:], a["mask_na"]).then_inc(mk_in, 16)
        pool.dma_start(rload[0:120, 0:31], a["rpb"][0].rearrange("h r c -> (h r) c")).then_inc(rp_in, 16)
        pool.wait_ge(rp_in, 16)
        pool.wait_ge(zeroed, 1)
        nc.gpsimd.tensor_copy(rpad[0:120, 48:79], backwards(rload[0:120, 0:31])).then_inc(zeroed, 1)
        pool.wait_ge(zeroed, 5)
        pool.dma_start(rpb_tab, rpad[0:120, :]).then_inc(rp_out, 16)
        pool.wait_ge(rp_out, 16)
        pool.wait_ge(mk_in, 16)
        maskq = maskna[:, 0:64].unsqueeze(1).to_broadcast([P, 8, 64])

        def head_bias(h):
            for r in range(4):
                src = bass.AP(rpb_tab.tensor, (15 * h + 7 - r) * 128, [[1, 64], [128, 4], [1, 64]])
                dst = bflip[64 * (r % 2):64 * (r % 2) + 64, r // 2, :].rearrange("p (i c) -> p i c", i=4)
                pool.dma_start(dst, src).then_inc(bias_in, 16)
            pool.wait_ge(bias_in, 64 * (h + 1))
            if h >= 1:
                pool.wait_ge(sm_ok, h)
            nc.gpsimd.tensor_tensor(bias[:].rearrange("p m (i c) -> p (m i) c", c=64),
                                    backwards(bflip[:].rearrange("p m (i c) -> p (m i) c", c=64)),
                                    maskq, ALU.add).then_inc(bias_ok, 1)
            pool.wait_ge(bias_ok, h + 1)

        head_bias(0)
        pool.wait_ge(cols_e, 2)
        pool.wait_ge(tlo, G0["z"] + 2)
        wide = [P, 2, T]
        nc.gpsimd.tensor_tensor(cacc[:, 6:8, :], zt[:, 6:8, 0:T], wdw[:, 6:8, 0:1].to_broadcast(wide),
                                ALU.mult).then_inc(ptap, 1)
        pool.wait_ge(ptap, 1)
        b_dw = gcol[:, GC["b_dw"] + 6:GC["b_dw"] + 8].unsqueeze(2).to_broadcast(wide)
        nc.gpsimd.tensor_tensor(cacc[:, 6:8, :], cacc[:, 6:8, :], b_dw, ALU.add).then_inc(ptap, 1)
        with pool.Fori(1, TAPS) as i:
            pool.wait_ge(ptap, i * 2)
            nc.gpsimd.tensor_tensor(ptmp[:], zt[:, 6:8, bass.ds(i, T)],
                                    wdw[:, 6:8, bass.ds(i, 1)].to_broadcast(wide), ALU.mult).then_inc(ptap, 1)
            pool.wait_ge(ptap, i * 2 + 1)
            nc.gpsimd.tensor_tensor(cacc[:, 6:8, :], cacc[:, 6:8, :], ptmp[:], ALU.add).then_inc(ptap, 1)
        for h in range(1, H):
            head_bias(h)

        pool.wait_ge(tsrc, G0["h1"] - 4)
        pool.dma_start(hres[:], x_v).then_inc(hres_in, 16)
        pool.dma_start(gpost[:], a["mix_post_g"].partition_broadcast(P)).then_inc(gp_in, 16)
        pool.wait_ge(tsrc, G0["f"] - 4)
        pool.dma_start(gpost[:], a["ffn_post_g"].partition_broadcast(P)).then_inc(gp_in, 16)
        pool.wait_ge(tsrc, G0["latent"] - 4)
        pool.dma_start(gpost[:], a["norm_attn_post_2"].partition_broadcast(P)).then_inc(gp_in, 16)
        pool.dma_start(masks[:, 0, :, :], a["log_count"].rearrange("(m p) k -> p m k", p=P)).then_inc(c2_in, 16)
        pool.dma_start(masks[:, 1, :, :], a["causal"].rearrange("(m p) k -> p m k", p=P)).then_inc(c2_in, 16)
        pool.dma_start(posi[:], a["positions_2"][0].rearrange("(m p) -> p m", p=P), allow_slow_non_contiguous=True).then_inc(c2_in, 16)
        pool.dma_start(invf[:], a["inv_freq"].partition_broadcast(P)).then_inc(c2_in, 16)

        def rope(x1, x2, f0, heads, r, step):
            n = heads * r
            for m in range(2):
                cos = ang[:, 0, m, f0:f0 + r].unsqueeze(1).to_broadcast([P, heads, r])
                sin = ang[:, 1, m, f0:f0 + r].unsqueeze(1).to_broadcast([P, heads, r])
                t = [rtmp[:, i, 0:n].rearrange("p (h r) -> p h r", r=r) for i in range(4)]
                if step[0]:
                    pool.wait_ge(rot, step[0])
                nc.gpsimd.tensor_tensor(t[0], x1[:, m], cos, ALU.mult)
                nc.gpsimd.tensor_tensor(t[1], x2[:, m], sin, ALU.mult)
                nc.gpsimd.tensor_tensor(t[2], x2[:, m], cos, ALU.mult)
                nc.gpsimd.tensor_tensor(t[3], x1[:, m], sin, ALU.mult).then_inc(rot, 1)
                pool.wait_ge(rot, step[0] + 1)
                nc.gpsimd.tensor_tensor(x1[:, m], t[0], t[1], ALU.subtract)
                nc.gpsimd.tensor_tensor(x2[:, m], t[2], t[3], ALU.add).then_inc(rot, 1)
                step[0] += 2

        def heads_view(buf, c0, width, lo_, r):
            return buf[:, :, c0:c0 + H * width].rearrange("p m (h w) -> p m h w", w=width)[:, :, :, lo_:lo_ + r]

        step = [0]
        pool.wait_ge(sin_ok, 2)
        pool.wait_ge(kr_e, 1)
        rope(kr[:, :, 0:32].unsqueeze(2), kr[:, :, 32:64].unsqueeze(2), 0, 1, 32, step)
        pool.wait_ge(a_free, A0["aq"] + 1)
        pool.wait_ge(b_free, B0["aq"] + 1)
        rope(heads_view(aqkv, 0, DH, 0, 16), heads_view(aqkv, 0, DH, 16, 16), 32, H, 16, step)
        pool.wait_ge(a_free, A0["up_lat"] + 2)
        pool.wait_ge(b_free, B0["up_lat"] + 1)
        rope(heads_view(uq, 0, 192, 128, 32), heads_view(uq, 0, 192, 160, 32), 0, H, 32, step)
        pool.wait_ge(a_free, A0["akv"] + 1)
        pool.wait_ge(b_free, B0["akv"] + 1)
        rope(heads_view(aqkv, 1024, DH, 0, 16), heads_view(aqkv, 1024, DH, 16, 16), 32, H, 16, step)
        pool.wait_ge(tsrc, G0["u0"] - 4)
        pool.dma_start(gpost[:], a["norm_mlp_post_2"].partition_broadcast(P)).then_inc(gp_in, 16)

    @block.scalar
    def _(act):
        def split(b, per=0, it=0):
            if b >= TOTAL:
                return
            act.wait_ge(raw_in[b % 4], raw_value(b, per, it))
            if b >= 4:
                act.wait_ge(used, b + per * it - 3)
            nc.scalar.activation(hi[:, b % 4, :], raw[:, b % 4, :], ACT.Copy).then_inc(hi_ready, 1)

        sums = [0]

        def square(src, dst, k):
            if sums[0] >= 2:
                act.wait_ge(acs, sums[0] - 1)
            nc.scalar.activation(dst, src, ACT.Square, accum_out=k).then_inc(acs, 1)
            sums[0] += 1

        def group_hi(g, dst, gain=None, when=None):
            act.wait_ge(tdone, g + 1 if when is None else when)
            if gain is None:
                nc.scalar.activation(flat(dst), flat(psT[:]), ACT.Copy).then_inc(thi, 1)
                return
            for j in range(4):
                ins = nc.scalar.activation(dst[:, j, :], psT[:, j // 2, T * (j % 2):T * (j % 2) + T], ACT.Copy,
                                           scale=gcol[:, gain + j:gain + j + 1])
            ins.then_inc(thi, 1)

        roots = [0]

        def root(k):
            act.wait_ge(var_ok, roots[0] + 1)
            nc.scalar.activation(stat[:, k, 1, :], stat[:, k, 0, :], ACT.Sqrt).then_inc(sq_ok, 1)
            roots[0] += 1

        def rstd(k, m):
            return stat[:, k, 3, m:m + 1]

        act.wait_ge(cols_e, 1)
        for g in range(4):
            group_hi(g, xh[:, 4 * g:4 * g + 4, :], GC["mix_pre_g"] + 4 * g)
            split(2 * g)
            split(2 * g + 1)
        for q in range(4):
            act.wait_ge(x_in[q], 16)
            for m in range(2):
                square(xin[:, m, N * q:N * q + N], sg[:, m, :], ssq[:, 0, m, q:q + 1])
        root(0)

        for j in range(2):
            b = C0["conv_in"] + 16 * j
            for c in range(16):
                if j == 1 and c == 1:
                    act.wait_ge(zeroed, 3)
                    act.wait_ge(tdone, G0["z"] + 1)
                    nc.scalar.activation(zt[:, 0:2, PAD:PAD + T], psT[:, 0, :].rearrange("p (a t) -> p a t", a=2),
                                         ACT.Copy).then_inc(thi, 1)
                if c == 7:
                    act.wait_ge(used, b + 8)
                    if j == 0:
                        act.wait_ge(rs_ok, 1)
                        act.wait_ge(acs, SUMS["x"])
                    else:
                        act.wait_ge(tsrc, 1)
                    for m in range(2):
                        ins = nc.scalar.activation(sg[:, m, :], psA[:, m, :], ACT.Sigmoid, scale=rstd(0, m))
                    ins.then_inc(a_free, 1)
                if j or c >= 4:
                    split(b + c + AHEAD)

        def qkv_pair(it, first):
            b = C0["qkv"]
            for c in range(16):
                if first and c == 1:
                    act.wait_ge(tdone, G0["z"] + 2)
                    nc.scalar.activation(zt[:, 4:6, PAD:PAD + T], psT[:, 0, :].rearrange("p (a t) -> p a t", a=2),
                                         ACT.Copy).then_inc(thi, 1)
                for half, ps, free in ((0, psA, a_free), (1, psB, b_free)):
                    if c == 7 + 8 * half:
                        act.wait_ge(used, b + 16 * it + c + 1)
                        for m in range(2):
                            ins = nc.scalar.activation(qkv[:, m, bass.ds(it * 1024 + N * half, N)], ps[:, m, :],
                                                       ACT.Copy, scale=rstd(0, m))
                        ins.then_inc(free, 1)
                split(b + c + AHEAD, 16, it)

        qkv_pair(0, True)
        with act.Fori(1, 3) as it:
            qkv_pair(it, False)

        def qk_out(n, dst, busy):
            act.wait_ge(qk_t, n + 1)
            if busy is not None:
                act.wait_ge(sc_ok, busy)
            return nc.scalar.activation(flat(dst[:]), ps6[:], ACT.Copy)

        def exps(n, prob):
            act.wait_ge(mx_ok, n + 1)
            if n >= 2:
                act.wait_ge(o_ok, n - 1)
            for m in range(2):
                ins = nc.scalar.activation(prob[:, m, :], prob[:, m, :], ACT.Exp, bias=nmx[:, m:m + 1],
                                           accum_out=rsum[:, n % 2, m:m + 1])
            ins.then_inc(ex_ok, 1)

        def p_out(n, pt, busy, ps=ps6[:]):
            act.wait_ge(p_t, n + 1)
            if busy is not None:
                act.wait_ge(pv_ok, busy)
            nc.scalar.activation(flat(pt[:]), ps, ACT.Copy).then_inc(p_e, 1)

        def o_high(n, dst, ps=ps6[:, 0:T]):
            act.wait_ge(o_t, n + 1)
            nc.scalar.activation(dst, ps, ACT.Copy).then_inc(o_hi, 1)

        for j in range(4):
            b = C0["gates"] + 16 * j
            for c in range(16):
                n, s = 2 * j + c // 8, c % 8
                if s == 0:
                    qk_out(n, qkt1, n if n else None).then_inc(qk_e, 1)
                if s == 3 and n:
                    o_high(n - 1, oh[:, n - 1, :])
                if s == 4:
                    exps(n, prob1)
                if s == 6:
                    p_out(n, pt1, n if n else None)
                if s == 7:
                    ps, free = (psA, a_free) if c < 8 else (psB, b_free)
                    act.wait_ge(used, b + c + 1)
                    for m in range(2):
                        ins = nc.scalar.activation(gates[:, m, 1024 * j + 64 * (c - 7):1024 * j + 64 * (c - 7) + N],
                                                   ps[:, m, :], ACT.Sigmoid, scale=rstd(0, m))
                    ins.then_inc(free, 1)
                if j == 2 and c == 2:
                    act.wait_ge(xc_ok, 1)
                    nc.scalar.activation(csq[:], cacc[:], ACT.Square).then_inc(csq_ok, 1)
                if j == 2 and c == 8:
                    act.wait_ge(cvv, 1)
                    nc.scalar.activation(st[:, 0, 1, 0:T], st[:, 0, 0, 0:T], ACT.Sqrt).then_inc(cvs, 1)
                if j == 2 and c == 13:
                    act.wait_ge(xn_ok, 1)
                    for t in range(8):
                        ins = nc.scalar.activation(cacc[:, t, :], cacc[:, t, :], ACT.Silu,
                                                   bias=gcol[:, GC["conv_ln_b"] + t:GC["conv_ln_b"] + t + 1],
                                                   scale=gcol[:, GC["conv_ln_g"] + t:GC["conv_ln_g"] + t + 1])
                    ins.then_inc(sil_ok, 1)
                if j == 3 and c == 1:
                    act.wait_ge(sil_ok, 1)
                    nc.scalar.activation(ch[:], cacc[:], ACT.Copy).then_inc(ch_ok, 1)
                split(b + c + AHEAD)
        o_high(7, oh[:, 7, :])

        def merge_pair(it, first):
            b = C0["merge"]
            for c in range(8):
                if not first and c == 1:
                    group_hi(0, xh[:, bass.ds(it * 4 - 4, 4), :], when=it + G0["merged"])
                split(b + c + AHEAD, 8, it)

        merge_pair(0, True)
        with act.Fori(1, 4) as it:
            merge_pair(it, False)

        def normed_pairs(name, per, k, before=None, begin=0, ends=None):
            ends = ends or [per // 2 - 1, per - 1, per + per // 2 - 1, 2 * per - 1]
            b = C0[name]
            for c in range(begin, 2 * per):
                if before is not None and c == 1:
                    before()
                if c in ends:
                    q = ends.index(c)
                    act.wait_ge(used, b + c + 1)
                    for m in range(2):
                        square((psA, psB)[q % 2][:, m, :], sg[:, m, :], ssq[:, k, m, q:q + 1])
                if c < 2 * per - 1:
                    split(b + c + AHEAD)
            root(k)

        def post(name, per, k, g0, gain):
            for i, q in enumerate(ORDER):
                group_hi(g0 + i, xh[:, 4 * q:4 * q + 4, :], gain + 4 * q)
                if i == 0:
                    split(C0[name] + 2 * per - 1 + AHEAD)
                else:
                    split(C0[name] + 2 * per + 2 * i - 2 + AHEAD)
                    split(C0[name] + 2 * per + 2 * i - 1 + AHEAD)
            for q in range(4):
                for m in range(2):
                    square(hres[:, m, N * q:N * q + N], sg[:, m, :], ssq[:, k, m, q:q + 1])
            root(k)

        normed_pairs("out1", 16, 1, lambda: group_hi(9, xh[:, 12:16, :]))
        post("out1", 16, 2, G0["h1"], GC["ffn_pre_g"])

        def ff1_pair(it, first):
            b = C0["ff1"]
            for c in range(6 if first else 0, 16):
                if not first and c == 1:
                    group_hi(0, fh[:, bass.ds(it * 4 - 4, 4), :], when=it + G0["f"])
                if c == 7:
                    act.wait_ge(used, b + 16 * it + 8)
                    if not first:
                        act.wait_ge(tsrc, it + G0["f"] - 4)
                    else:
                        act.wait_ge(acs, SUMS["h1"])
                        act.wait_ge(rs_ok, 3)
                    for m in range(2):
                        ins = nc.scalar.activation(sg[:, m, :], psA[:, m, :], ACT.Silu, scale=rstd(2, m))
                    ins.then_inc(a_free, 1)
                split(b + c + AHEAD, 16, it)

        ff1_pair(0, True)
        with act.Fori(1, 11) as it:
            ff1_pair(it, False)

        normed_pairs("down1", 44, 3, lambda: group_hi(24, fh[:, 40:44, :]))
        post("down1", 44, 4, G0["h2"], GC["norm_attn_pre_2"])

        b = C0["latent"]
        for c in range(6, 16):
            split(b + c + AHEAD)
        act.wait_ge(ang_ok, 1)
        nc.scalar.activation(ang[:, 1, :, :], ang[:, 3, :, :], ACT.Sin).then_inc(sin_ok, 1)
        nc.scalar.activation(ang[:, 0, :, :], ang[:, 4, :, :], ACT.Sin).then_inc(sin_ok, 1)
        split(C0["krope"] + AHEAD)

        def aqkv_half(b, c, p):
            for half, ps, free in ((0, psA, a_free), (1, psB, b_free)):
                if c == 7 + 8 * half:
                    act.wait_ge(used, b + c + 1)
                    for m in range(2):
                        ins = nc.scalar.activation(aqkv[:, m, 1024 * p + N * half:1024 * p + N * half + N],
                                                   ps[:, m, :], ACT.Copy, scale=rstd(4, m))
                    ins.then_inc(free, 1)

        for c in range(16):
            if c == 1:
                act.wait_ge(tsrc, G0["h3"] - 4)
                for k in range(2):
                    for m in range(2):
                        square(st[:, k, m, :], sg[:, m, :], ssq[:, 5 + k, m, 0:1])
                group_hi(29, lh[:, 0:4, :], GC["q_latent_norm_2"])
            if c == 3:
                group_hi(30, lh[:, 4:8, :], GC["kv_latent_norm_2"])
                root(5)
                root(6)
            if c == 7:
                act.wait_ge(rs_ok, 5)
            aqkv_half(C0["aq"], c, 0)
            split(C0["aq"] + c + AHEAD)
        act.wait_ge(rs_ok, 7)
        for i in range(7):
            ps, free = (psA, a_free) if i % 2 == 0 else (psB, b_free)
            dst, c, k = (uq, N * i, 5) if i < 3 else (ukv, N * (i - 3), 6)
            split(C0["up_lat"] + 2 * i + AHEAD)
            act.wait_ge(used, C0["up_lat"] + 2 * i + 2)
            for m in range(2):
                ins = nc.scalar.activation(dst[:, m, c:c + N], ps[:, m, :], ACT.Copy, scale=rstd(k, m))
            ins.then_inc(free, 1)
            split(C0["up_lat"] + 2 * i + 1 + AHEAD)

        def heads_slot(slot):
            for n in head_steps(slot, 5):
                o_high(n, lh[:, n - 8, :] if n < 16 else xh[:, n - 16, :], psT[:, 0, T:2 * T])
            for n in head_steps(slot, 3):
                p_out(n, pt2, n, psT[:, 1, :])
            for n in head_steps(slot, 2):
                exps(n, prob2)
            for n in head_steps(slot, 0):
                ins = qk_out(n, qkt2, n)
                if n < 16:
                    ins = nc.scalar.activation(qrt[:], psT[0:ROPE_B, 0, T:2 * T], ACT.Copy)
                ins.then_inc(qk_e, 1)

        act.wait_ge(kr_t, 1)
        nc.scalar.activation(krt[:], psT[0:ROPE_B, 0, 0:T], ACT.Copy).then_inc(krt_ok, 1)
        for c in range(32):
            heads_slot(c)
            aqkv_half(C0["akv"] + c // 16 * 16, c % 16, 1 + c // 16)
            split(C0["akv"] + c + AHEAD)
        for c in range(16):
            heads_slot(32 + c)
            for half, ps, free in ((0, psA, a_free), (1, psB, b_free)):
                if c == 3 + 4 * half:
                    act.wait_ge(used, C0["out2"] + c + 1)
                    nc.scalar.activation(ukv[:, :, N * half:N * half + N], ps[:], ACT.Copy).then_inc(free, 1)
            split(C0["out2"] + c + AHEAD)
        normed_pairs("out2", 16, 7, begin=16, ends=[19, 23, 27, 31])
        post("out2", 16, 8, G0["h3"], GC["norm_mlp_pre_2"])

        def up_pair(name, it, first, g0, start):
            b = C0[name]
            for c in range(start if first else 0, 16):
                if not first and c == 1:
                    group_hi(0, uh[:, bass.ds(it * 8 - 4, 4), :], when=it * 2 + g0)
                if c == 9:
                    group_hi(0, uh[:, bass.ds(it * 8, 4), :], when=it * 2 + g0 + 1)
                for half, ps, free in ((0, psA, a_free), (1, psB, b_free)):
                    if c == 7 + 8 * half:
                        act.wait_ge(used, b + 16 * it + c + 1)
                        act.wait_ge(tdone, it * 2 + g0 + half - 1)
                        if first:
                            act.wait_ge(rs_ok, 9)
                        for m in range(2):
                            ins = nc.scalar.activation(st[:, half, m, :], ps[:, m, :], ACT.Relu, scale=rstd(8, m))
                        ins.then_inc(free, 1)
                split(b + c + AHEAD, 16, it)

        def square_sum(q):
            act.wait_ge(acc_ok, q + 1)
            for m in range(2):
                square(acc[:, m, N * q:N * q + N], sg[:, m, :], ssq[:, 9, m, q:q + 1])

        def down_pairs(name, g_last, last=False):
            for j in range(2):
                for c in range(32):
                    if j == 0 and c == 1:
                        group_hi(g_last, uh[:, 28:32, :])
                    if last and 32 * j + c in (16, 32, 48):
                        square_sum(2 * j + c // 16 - 1)
                    split(C0[name] + 32 * j + c + AHEAD)

        up_pair("up2a", 0, True, G0["u0"], 6)
        with act.Fori(1, 4) as it:
            up_pair("up2a", it, False, G0["u0"], 0)
        down_pairs("down2a", G0["u0"] + 7)
        up_pair("up2b", 0, True, G0["u1"], 0)
        with act.Fori(1, 4) as it:
            up_pair("up2b", it, False, G0["u1"], 0)
        down_pairs("down2b", G0["u1"] + 7, last=True)
        square_sum(3)
        root(9)

    @block.vector
    def _(v):
        chain = [0]

        def link(ins):
            chain[0] += 1
            ins.then_inc(vec, 1)
            v.wait_ge(vec, chain[0])

        def split(b, per=0, it=0):
            if b >= TOTAL:
                return
            v.wait_ge(hi_ready, b + per * it + 1)
            nc.vector.tensor_tensor(lo[:, b % 4, :], raw[:, b % 4, :], hi[:, b % 4, :].bitcast(F32),
                                    ALU.subtract).then_inc(lo_ready, 1)

        def group_lo(g, dst_l, dst_h, gain=None, when=None):
            v.wait_ge(thi, g + 1 if when is None else when)
            if gain is None:
                nc.vector.tensor_tensor(flat(dst_l), flat(psT[:]), flat(dst_h).bitcast(F32),
                                        ALU.subtract).then_inc(tlo, 1)
                return
            for j in range(4):
                ins = nc.vector.scalar_tensor_tensor(
                    out=dst_l[:, j, :], in0=psT[:, j // 2, T * (j % 2):T * (j % 2) + T],
                    scalar=gcol[:, gain + j:gain + j + 1], in1=dst_h[:, j, :].bitcast(F32),
                    op0=ALU.mult, op1=ALU.subtract)
            ins.then_inc(tlo, 1)

        roots = [0]

        def variance(k, width, parts, need):
            v.wait_ge(acs, need)
            link(nc.vector.tensor_reduce(stat[:, k, 1, :], ssq[:, k, :, 0:parts], AX_X, ALU.add))
            nc.vector.tensor_scalar(stat[:, k, 0, :], stat[:, k, 1, :], 1.0 / width, EPS, ALU.mult,
                                    ALU.add).then_inc(var_ok, 1)

        def inverse_root(var, root_, y, t, dst):
            link(nc.vector.reciprocal(y, root_))
            link(nc.vector.tensor_tensor(t, y, y, ALU.mult))
            link(nc.vector.tensor_tensor(t, t, var, ALU.mult))
            link(nc.vector.tensor_scalar(t, t, -0.5, 1.5, ALU.mult, ALU.add))
            return nc.vector.tensor_tensor(dst, y, t, ALU.mult)

        def finish(k):
            v.wait_ge(sq_ok, roots[0] + 1)
            roots[0] += 1
            inverse_root(stat[:, k, 0, :], stat[:, k, 1, :], stat[:, k, 2, :], stat[:, k, 1, :],
                         stat[:, k, 3, :]).then_inc(rs_ok, 1)
            v.wait_ge(rs_ok, roots[0])

        def rstd(k, m):
            return stat[:, k, 3, m:m + 1]

        v.wait_ge(cols_t, 1)
        nc.vector.tensor_copy(gcol[:, 0:FIRST], ps7[:, 0:FIRST]).then_inc(cols_e, 1)
        v.wait_ge(cols_e, 1)
        for g in range(4):
            group_lo(g, xl[:, 4 * g:4 * g + 4, :], xh[:, 4 * g:4 * g + 4, :], GC["mix_pre_g"] + 4 * g)
            split(2 * g)
            split(2 * g + 1)
        variance(0, D, 4, SUMS["x"])
        finish(0)

        def z_out(g, t):
            v.wait_ge(thi, g + 1)
            v.wait_ge(zeroed, 3)
            nc.vector.tensor_copy(zt[:, t:t + 2, PAD:PAD + T],
                                  psT[:, 1, :].rearrange("p (a t) -> p a t", a=2)).then_inc(tlo, 1)

        for j in range(2):
            b = C0["conv_in"] + 16 * j
            for c in range(16):
                if j == 1 and c == 1:
                    z_out(G0["z"], 2)
                if j == 1 and c == 3:
                    v.wait_ge(cols_t, 2)
                    nc.vector.tensor_copy(gcol[:, FIRST:], ps7[:, FIRST:NGAIN])
                    nc.vector.tensor_copy(flat(wdw[:]), ps6[:, 0:256]).then_inc(cols_e, 1)
                if c == 15:
                    v.wait_ge(used, b + 16)
                    v.wait_ge(a_free, A0["conv_in"] + j + 1)
                    for m in range(2):
                        ins = nc.vector.scalar_tensor_tensor(out=st[:, j, m, :], in0=psB[:, m, :],
                                                             scalar=rstd(0, m), in1=sg[:, m, :],
                                                             op0=ALU.mult, op1=ALU.mult)
                    ins.then_inc(tsrc, 1)
                if j or c >= 4:
                    split(b + c + AHEAD)

        def conv_taps(slot):
            if slot >= 2 * TAPS:
                return
            i = slot % TAPS
            for r in range(3):
                ct = 3 * (slot // TAPS) + r
                if i == 0:
                    c = GC["b_dw"] + ct
                    nc.vector.tensor_scalar(cacc[:, ct, :], zt[:, ct, 0:T], wdw[:, ct, 0:1], gcol[:, c:c + 1],
                                            ALU.mult, ALU.add).then_inc(tap, 1)
                else:
                    v.wait_ge(tap, 3 * slot + r - 2)
                    nc.vector.scalar_tensor_tensor(out=cacc[:, ct, :], in0=zt[:, ct, i:i + T],
                                                   scalar=wdw[:, ct, i:i + 1], in1=cacc[:, ct, :], op0=ALU.mult,
                                                   op1=ALU.add).then_inc(tap, 1)

        v.wait_ge(cols_e, 2)
        for c in range(48):
            if c == 1:
                z_out(G0["z"] + 1, 6)
            if c == 2:
                v.wait_ge(tlo, G0["z"] + 2)
            conv_taps(c)
            split(C0["qkv"] + c + AHEAD)

        def softmax(n, prob, scale, bias_, first=False):
            v.wait_ge(sc_ok, n + 1)
            if not first:
                v.wait_ge(p_t, n)
            nc.vector.scalar_tensor_tensor(out=flat(prob[:]), in0=ps7[:], scalar=scale, in1=bias_,
                                           op0=ALU.mult, op1=ALU.add).then_inc(sm_ok, 1)
            v.wait_ge(sm_ok, n + 1)
            nc.vector.tensor_reduce(nmx[:], prob[:], AX_X, ALU.max, negate=True).then_inc(mx_ok, 1)

        def o_out(n, ost, first=False, ps=ps7):
            v.wait_ge(pv_ok, n + 1)
            if not first:
                v.wait_ge(o_t, n)
            nc.vector.reciprocal(rinv[:], rsum[:, n % 2, :]).then_inc(ri_ok, 1)
            v.wait_ge(ri_ok, n + 1)
            for m in range(2):
                ins = nc.vector.tensor_scalar(ost[:, m, :], ps[:, DH * m:DH * m + DH], rinv[:, m:m + 1],
                                              None, ALU.mult)
            ins.then_inc(o_ok, 1)

        def o_low(n, dst_l, dst_h, ps=ps6[:, 0:T]):
            v.wait_ge(o_hi, n + 1)
            nc.vector.tensor_tensor(dst_l, ps, dst_h.bitcast(F32), ALU.subtract).then_inc(o_lo, 1)

        cv, cs_, cy, ct_ = (st[:, i // 2, i % 2, 0:T] for i in range(4))
        for j in range(4):
            for c in range(16):
                n, s = 2 * j + c // 8, c % 8
                if s == 2:
                    v.wait_ge(bias_ok, n + 1)
                    softmax(n, prob1, SCALE_A, flat(bias[:]), first=(n == 0))
                if s == 3 and n:
                    o_low(n - 1, ol[:, n - 1, :], oh[:, n - 1, :])
                if s == 7:
                    o_out(n, ost1, first=(n == 0))
                conv_taps(48 + 16 * j + c)
                if j == 2 and c == 1:
                    v.wait_ge(mu_ok, 1)
                    v.wait_ge(tap, 6 * TAPS)
                    v.wait_ge(ptap, 2 * TAPS)
                    nc.vector.tensor_tensor(cacc[:], cacc[:], psT[:, 0, 0:T].unsqueeze(1).to_broadcast([P, 8, T]),
                                            ALU.subtract).then_inc(xc_ok, 1)
                if j == 2 and c == 7:
                    v.wait_ge(cv_ok, 1)
                    nc.vector.tensor_scalar(cv, psT[:, 1, 0:T], EPS, None, ALU.add).then_inc(cvv, 1)
                if j == 2 and c == 9:
                    v.wait_ge(cvs, 1)
                    link(inverse_root(cv, cs_, cy, ct_, cs_))
                if j == 2 and c == 11:
                    v.wait_ge(csq_ok, 1)
                    nc.vector.tensor_tensor(cacc[:], cacc[:], cs_.unsqueeze(1).to_broadcast([P, 8, T]),
                                            ALU.mult).then_inc(xn_ok, 1)
                if j == 3 and c == 3:
                    v.wait_ge(ch_ok, 1)
                    nc.vector.tensor_tensor(cl[:], cacc[:], ch[:].bitcast(F32), ALU.subtract).then_inc(cl_ok, 1)
                split(C0["gates"] + 16 * j + c + AHEAD)
        o_low(7, ol[:, 7, :], oh[:, 7, :])

        def merge_pair(it, first):
            b = C0["merge"]
            for c in range(8):
                if not first and c == 1:
                    group_lo(0, xl[:, bass.ds(it * 4 - 4, 4), :], xh[:, bass.ds(it * 4 - 4, 4), :],
                             when=it + G0["merged"])
                if c == 3:
                    v.wait_ge(used, b + 8 * it + 4)
                    for m in range(2):
                        ins = nc.vector.tensor_tensor(sg[:, m, :], psA[:, m, :], gates[:, m, bass.ds(it * N, N)],
                                                      ALU.mult)
                    ins.then_inc(a_free, 1)
                if c == 7:
                    v.wait_ge(used, b + 8 * it + 8)
                    if not first:
                        v.wait_ge(tdone, it + G0["merged"])
                    v.wait_ge(a_free, it + A0["merge"] + 1)
                    for m in range(2):
                        ins = nc.vector.tensor_tensor(st[:, 0, m, :], psB[:, m, :],
                                                      gates[:, m, bass.ds(it * N + D, N)], ALU.mult)
                    ins.then_inc(mrg, 1)
                    v.wait_ge(mrg, it + 1)
                    nc.vector.tensor_tensor(st[:, 0, :, :], st[:, 0, :, :], sg[:], ALU.add).then_inc(tsrc, 1)
                split(b + c + AHEAD, 8, it)

        merge_pair(0, True)
        with v.Fori(1, 4) as it:
            merge_pair(it, False)

        def normed_pairs(name, per, k, gains_in, last_group=None, begin=0, ends=None):
            ends = ends or [per // 2 - 1, per - 1]
            need = SUMS[name] - 8
            b = C0[name]
            for c in range(begin, 2 * per):
                if c == 1 and last_group is not None:
                    last_group()
                if c in ends:
                    half = ends.index(c)
                    v.wait_ge(acs, need + 2 * half + 2)
                    if half == 0:
                        v.wait_ge(gp_in, gains_in)
                    ps, free = ((psA, a_free), (psB, b_free))[half]
                    for m in range(2):
                        ins = nc.vector.tensor_tensor(st[:, half, m, :], ps[:, m, :],
                                                      gpost[:, N * half:N * half + N], ALU.mult)
                    ins.then_inc(free, 1)
                if c < 2 * per - 1:
                    split(b + c + AHEAD)
            variance(k, D, 4, SUMS[name])
            finish(k)

        def post(name, per, k, k_next, g0, gain, sums):
            def low(i):
                q = ORDER[i]
                group_lo(g0 + i, xl[:, 4 * q:4 * q + 4, :], xh[:, 4 * q:4 * q + 4, :], gain + 4 * q)

            def make(i):
                q = ORDER[i]
                if q >= 2:
                    ps = psA if q == 2 else psB
                    if i:
                        v.wait_ge(tsrc, g0 + i - 4)
                    for m in range(2):
                        ins = nc.vector.scalar_tensor_tensor(out=sg[:, m, :], in0=ps[:, m, :], scalar=rstd(k, m),
                                                             in1=gpost[:, N * q:N * q + N], op0=ALU.mult,
                                                             op1=ALU.mult)
                    link(ins)
                    nc.vector.tensor_tensor(hres[:, :, N * q:N * q + N], hres[:, :, N * q:N * q + N], sg[:],
                                            ALU.add).then_inc(tsrc, 1)
                else:
                    for m in range(2):
                        ins = nc.vector.scalar_tensor_tensor(out=hres[:, m, N * q:N * q + N], in0=st[:, q, m, :],
                                                             scalar=rstd(k, m), in1=hres[:, m, N * q:N * q + N],
                                                             op0=ALU.mult, op1=ALU.add)
                    ins.then_inc(tsrc, 1)

            c = C0[name] + 2 * per + AHEAD
            make(0)
            make(1)
            low(0)
            split(c - 1)
            for i in (1, 2, 3):
                if i < 3:
                    make(i + 1)
                low(i)
                split(c + 2 * i - 2)
                split(c + 2 * i - 1)
            variance(k_next, D, 4, sums)
            finish(k_next)

        normed_pairs("out1", 16, 1, 16, lambda: group_lo(9, xl[:, 12:16, :], xh[:, 12:16, :]))
        v.wait_ge(hres_in, 16)
        post("out1", 16, 1, 2, G0["h1"], GC["ffn_pre_g"], SUMS["h1"])

        def ff1_pair(it, first):
            b = C0["ff1"]
            for c in range(6 if first else 0, 16):
                if not first and c == 1:
                    group_lo(0, fl[:, bass.ds(it * 4 - 4, 4), :], fh[:, bass.ds(it * 4 - 4, 4), :],
                             when=it + G0["f"])
                if c == 15:
                    v.wait_ge(used, b + 16 * it + 16)
                    v.wait_ge(a_free, it + A0["ff1"] + 1)
                    if not first:
                        v.wait_ge(tdone, it + G0["f"])
                    for m in range(2):
                        ins = nc.vector.scalar_tensor_tensor(out=st[:, 0, m, :], in0=psB[:, m, :],
                                                             scalar=rstd(2, m), in1=sg[:, m, :],
                                                             op0=ALU.mult, op1=ALU.mult)
                    ins.then_inc(tsrc, 1)
                split(b + c + AHEAD, 16, it)

        ff1_pair(0, True)
        with v.Fori(1, 11) as it:
            ff1_pair(it, False)

        normed_pairs("down1", 44, 3, 32, lambda: group_lo(24, fl[:, 40:44, :], fh[:, 40:44, :]))
        post("down1", 44, 3, 4, G0["h2"], GC["norm_attn_pre_2"], SUMS["h2"])

        def angles():
            v.wait_ge(c2_in, 64)
            link(nc.vector.tensor_copy(posf[:], posi[:]))
            for m in range(2):
                ins = nc.vector.tensor_scalar(ang[:, 2, m, :], invf[:], posf[:, m:m + 1], None, ALU.mult)
            link(ins)
            big = 12582912.0
            turns, r, rc = flat(ang[:, 3, :, :]), flat(ang[:, 2, :, :]), flat(ang[:, 4, :, :])
            link(nc.vector.tensor_scalar(turns, r, 1.0 / TWO_PI, big, ALU.mult, ALU.add))
            link(nc.vector.tensor_scalar(turns, turns, -big, None, ALU.add))
            p1, p2 = 6.28125, 0.0019340515136718750
            p3 = TWO_PI - p1 - p2
            for part in (p1, p2, p3):
                link(nc.vector.scalar_tensor_tensor(out=r, in0=turns, scalar=-part, in1=r, op0=ALU.mult,
                                                    op1=ALU.add))
            link(nc.vector.tensor_scalar(turns, r, PI_LO, -PI_LO, ALU.min, ALU.max))
            link(nc.vector.tensor_scalar(rc, r, TWO_PI / 4, None, ALU.add))
            link(nc.vector.tensor_scalar(r, rc, TWO_PI / 2, -TWO_PI, ALU.is_gt, ALU.mult))
            link(nc.vector.tensor_tensor(rc, rc, r, ALU.add))
            nc.vector.tensor_scalar(rc, rc, PI_LO, -PI_LO, ALU.min, ALU.max).then_inc(ang_ok, 1)

        for c in range(6, 16):
            for half, ps in ((0, psA), (1, psB)):
                if c == 7 + 8 * half:
                    v.wait_ge(used, C0["latent"] + c + 1)
                    for m in range(2):
                        ins = nc.vector.tensor_scalar(st[:, half, m, :], ps[:, m, :], rstd(4, m), None, ALU.mult)
                    ins.then_inc(tsrc, 1)
            if c == 9:
                angles()
            split(C0["latent"] + c + AHEAD)
        v.wait_ge(used, C0["krope"] + 1)
        for m in range(2):
            ins = nc.vector.tensor_scalar(kr[:, m, :], ps6[:, ROPE_B * m:ROPE_B * m + ROPE_B], rstd(4, m), None,
                                          ALU.mult)
        ins.then_inc(kr_e, 1)
        split(C0["krope"] + AHEAD)

        for c in range(16):
            if c == 1:
                group_lo(29, ll[:, 0:4, :], lh[:, 0:4, :], GC["q_latent_norm_2"])
            if c == 3:
                group_lo(30, ll[:, 4:8, :], lh[:, 4:8, :], GC["kv_latent_norm_2"])
                variance(5, RANK, 1, SUMS["latent"])
                variance(6, RANK, 1, SUMS["latent"])
                finish(5)
                finish(6)
            split(C0["aq"] + c + AHEAD)
        for c in range(14):
            split(C0["up_lat"] + c + AHEAD)

        def heads_slot(slot):
            for n in head_steps(slot, 5):
                o_low(n, ll[:, n - 8, :] if n < 16 else xl[:, n - 16, :],
                      lh[:, n - 8, :] if n < 16 else xh[:, n - 16, :], psT[:, 0, T:2 * T])
            for n in head_steps(slot, 4):
                o_out(n, ost2, ps=psT[:, 0, :])
            for n in head_steps(slot, 1):
                latent_ = n < 16
                softmax(n, prob2, SCALE_B if latent_ else SCALE_A, flat(masks[:, int(latent_), :, :]))

        for c in range(48):
            heads_slot(c)
            split(C0["akv"] + c + AHEAD)
        normed_pairs("out2", 16, 7, 48, begin=16, ends=[19, 23])
        post("out2", 16, 7, 8, G0["h3"], GC["norm_mlp_pre_2"], SUMS["h3"])

        def up_pair(name, it, first, g0, start):
            b = C0[name]
            for c in range(start if first else 0, 16):
                if not first and c == 1:
                    group_lo(0, ul[:, bass.ds(it * 8 - 4, 4), :], uh[:, bass.ds(it * 8 - 4, 4), :],
                             when=it * 2 + g0)
                if c == 9:
                    group_lo(0, ul[:, bass.ds(it * 8, 4), :], uh[:, bass.ds(it * 8, 4), :], when=it * 2 + g0 + 1)
                for half, free, f0 in ((0, a_free, A0[name]), (1, b_free, B0[name])):
                    if c == 7 + 8 * half:
                        v.wait_ge(free, it + f0 + 1)
                        nc.vector.tensor_tensor(st[:, half, :, :], st[:, half, :, :], st[:, half, :, :],
                                                ALU.mult).then_inc(tsrc, 1)
                split(b + c + AHEAD, 16, it)

        def gained(q):
            v.wait_ge(acs, SUMS["h3"] + 2 * q + 2)
            v.wait_ge(gp_in, 64)
            for m in range(2):
                part = acc[:, m, N * q:N * q + N]
                nc.vector.tensor_tensor(part, part, gpost[:, N * q:N * q + N], ALU.mult)

        def down_pairs(name, g_last, add):
            for j in range(2):
                b = C0[name] + 32 * j
                for c in range(32):
                    if j == 0 and c == 1:
                        group_lo(g_last, ul[:, 28:32, :], uh[:, 28:32, :])
                    if add and 32 * j + c in (17, 33, 49):
                        gained(2 * j + c // 16 - 1)
                    for half, ps, free in ((0, psA, a_free), (1, psB, b_free)):
                        if c == 15 + 16 * half:
                            v.wait_ge(used, b + c + 1)
                            dst = acc[:, :, N * (2 * j + half):N * (2 * j + half) + N]
                            if add:
                                nc.vector.tensor_tensor(dst, dst, ps[:], ALU.add).then_inc(acc_ok, 1)

                            else:
                                nc.vector.tensor_copy(dst, ps[:]).then_inc(free, 1)
                    split(b + c + AHEAD)

        up_pair("up2a", 0, True, G0["u0"], 6)
        with v.Fori(1, 4) as it:
            up_pair("up2a", it, False, G0["u0"], 0)
        down_pairs("down2a", G0["u0"] + 7, False)
        up_pair("up2b", 0, True, G0["u1"], 0)
        with v.Fori(1, 4) as it:
            up_pair("up2b", it, False, G0["u1"], 0)
        down_pairs("down2b", G0["u1"] + 7, True)
        variance(9, D, 4, SUMS["down2"])
        finish(9)
        for m in range(2):
            part = acc[:, m, 3 * N:]
            ins = nc.vector.scalar_tensor_tensor(out=part, in0=part, scalar=rstd(9, m), in1=gpost[:, 3 * N:],
                                                 op0=ALU.mult, op1=ALU.mult)
        link(ins)
        nc.vector.tensor_tensor(hres[:, :, 3 * N:], hres[:, :, 3 * N:], acc[:, :, 3 * N:], ALU.add).then_inc(tsrc, 1)
        for q in range(3):
            for m in range(2):
                part = hres[:, m, N * q:N * q + N]
                ins = nc.vector.scalar_tensor_tensor(out=part, in0=acc[:, m, N * q:N * q + N], scalar=rstd(9, m),
                                                     in1=part, op0=ALU.mult, op1=ALU.add)
            ins.then_inc(tsrc, 1)

    @block.tensor
    def _(pe):
        def chunk(out_, x_h, x_l, kts, first, last, b, per=0, it=0):
            pe.wait_ge(lo_ready, b + per * it + 1)
            for i, k in enumerate(kts):
                w_h, w_l = hi[:, b % 4, N * i:N * i + N], lo[:, b % 4, N * i:N * i + N]
                for m in range(2):
                    s_h, s_l = x_h[:, k, P * m:P * m + P], x_l[:, k, P * m:P * m + P]
                    nc.tensor.matmul(out_[:, m, :], s_h, w_h, start=(first and i == 0), stop=False)
                    nc.tensor.matmul(out_[:, m, :], s_h, w_l, start=False, stop=False)
                    ins = nc.tensor.matmul(out_[:, m, :], s_l, w_h, start=False, stop=(last and i == 1))
            ins.then_inc(used, 1)

        def group_t(g, src, when=None):
            if not (isinstance(g, int) and g == 0):
                pe.wait_ge(tlo, g)
            if when is not None:
                pe.wait_ge(tsrc, when)
            for j in range(4):
                for m in range(2):
                    ins = nc.tensor.transpose(psT[:, j // 2, T * (j % 2) + P * m:T * (j % 2) + P * m + P],
                                              src[:, m, P * j:P * j + P], ident[:])
            ins.then_inc(tdone, 1)

        def pair(b, per, it, x_h, x_l, a_wait, b_wait, hook=None, perm=None, start=None):
            half = per // 2
            for c in range(per):
                if start is not None:
                    start(c)
                for first, ps, wait in ((0, psA, a_wait), (half, psB, b_wait)):
                    if c == first and wait is not None:
                        pe.wait_ge(*wait)
                k = c % half
                kk = 2 * (perm[k] if perm else k)
                chunk(psB if c >= half else psA, x_h, x_l, (kk, kk + 1), k == 0, k == half - 1, b + c,
                      per, it)
                if hook is not None:
                    hook(c)

        pe.wait_ge(id_in, 16)
        pe.wait_ge(x_in[0], 16)
        group_t(0, xin[:, :, 0:N])
        pe.wait_ge(g1_in, 16)
        nc.tensor.transpose(ps7[:, 0:FIRST], gload[0:FIRST, :], ident[0:FIRST, 0:FIRST]).then_inc(cols_t, 1)

        def x_start(c):
            if c % 2 == 0 and c < 8:
                g = c // 2
                pe.wait_ge(tlo, g + 1)
                if g < 3:
                    pe.wait_ge(x_in[g + 1], 16)
                    group_t(g + 1, xin[:, :, N * g + N:N * g + 2 * N])

        def z_hook(g):
            return lambda c: group_t(g, st[:, g - G0["z"], :, :], when=g - 3) if c == 1 else None

        pair(C0["conv_in"], 16, 0, xh, xl, None, None, start=x_start)
        pe.wait_ge(gl_in, 16 * (len(GAINS) - 1))
        pe.wait_ge(dw_in, 16)
        nc.tensor.transpose(ps7[:, 0:NGAIN], gload[0:NGAIN, :], ident[0:NGAIN, 0:NGAIN])
        for t in range(8):
            ins = nc.tensor.transpose(ps6[:, 32 * t:32 * t + 32], dwload[:, P * t:P * t + P], ident[0:32, 0:32])
        ins.then_inc(cols_t, 1)
        pair(C0["conv_in"] + 16, 16, 0, xh, xl, (a_free, 1), (tsrc, 1), z_hook(4))
        pair(C0["qkv"], 16, 0, xh, xl, (a_free, A0["qkv"]), (tsrc, 2), z_hook(5))
        with pe.Fori(1, 3) as it:
            pair(C0["qkv"], 16, it, xh, xl, (a_free, it + A0["qkv"]), (b_free, it + B0["qkv"]))

        def qk_turn(n, q_of, k_of, bank6):
            if bank6 is not None:
                pe.wait_ge(*bank6)
            for i, of in enumerate((q_of, k_of)):
                for m in range(2):
                    ins = nc.tensor.transpose(ps6[:, T * i + P * m:T * i + P * m + P], of(m), ident[:])
            return ins

        def scores(n, qkt, bank7, rope_=False):
            pe.wait_ge(qk_e, n + 1)
            if bank7 is not None:
                pe.wait_ge(*bank7)
            for m in range(2):
                ins = nc.tensor.matmul(ps7[:, T * m:T * m + T], qkt[:, 0, P * m:P * m + P], qkt[:, 1, :],
                                       start=True, stop=not rope_)
                if rope_:
                    ins = nc.tensor.matmul(ps7[:, T * m:T * m + T], qrt[:, P * m:P * m + P], krt[:],
                                           start=False, stop=True)
            ins.then_inc(sc_ok, 1)

        def p_turn(n, prob, ps, free):
            pe.wait_ge(ex_ok, n + 1)
            if free is not None:
                pe.wait_ge(*free)
            for k in range(2):
                for m in range(2):
                    ins = nc.tensor.transpose(ps[:, T * k + P * m:T * k + P * m + P], prob[:, m, P * k:P * k + P],
                                              ident[:])
            ins.then_inc(p_t, 1)

        def values(n, pt, ps, v_of, free=None):
            pe.wait_ge(p_e, n + 1)
            if free is not None:
                pe.wait_ge(*free)
            for m in range(2):
                for k in range(2):
                    ins = nc.tensor.matmul(ps[:, DH * m:DH * m + DH], pt[:, k, P * m:P * m + P], v_of(k),
                                           start=(k == 0), stop=(k == 1))
            ins.then_inc(pv_ok, 1)

        def o_turn(n, ost, ps, free):
            pe.wait_ge(o_ok, n + 1)
            if free is not None:
                pe.wait_ge(*free)
            for m in range(2):
                ins = nc.tensor.transpose(ps[:, P * m:P * m + P], ost[:, m, :], ident[:])
            ins.then_inc(o_t, 1)

        for j in range(4):
            def hook(c, j=j):
                n, s = 2 * j + c // 8, c % 8
                if s == 0:
                    if n == 0:
                        pe.wait_ge(b_free, B0["gates"])
                    qk_turn(n, lambda m: qkv[:, m, DH * n:DH * n + DH],
                            lambda m: qkv[:, m, 1024 + DH * n:1024 + DH * n + DH],
                            (p_e, n) if n else None).then_inc(qk_t, 1)
                if s == 2:
                    scores(n, qkt1, (o_ok, n) if n else None)
                if s == 3 and n:
                    o_turn(n - 1, ost1, ps6, (qk_e, n + 1))
                if s == 5:
                    p_turn(n, prob1, ps6, (o_lo, n) if n else None)
                if s == 7:
                    values(n, pt1, ps7, lambda k: qkv[:, k, 2048 + DH * n:2048 + DH * n + DH])
                if j == 2 and c == 0:
                    pe.wait_ge(tap, 6 * TAPS)
                    pe.wait_ge(ptap, 2 * TAPS)
                    pe.wait_ge(tlo, G0["merged"])
                    pe.wait_ge(zeroed, 4)
                    for t in range(8):
                        ins = nc.tensor.matmul(psT[:, 0, 0:T], ones[:], cacc[:, t, :], start=(t == 0),
                                               stop=(t == 7))
                    ins.then_inc(mu_ok, 1)
                if j == 2 and c == 5:
                    pe.wait_ge(csq_ok, 1)
                    for t in range(8):
                        ins = nc.tensor.matmul(psT[:, 1, 0:T], ones[:], csq[:, t, :], start=(t == 0),
                                               stop=(t == 7))
                    ins.then_inc(cv_ok, 1)

            pair(C0["gates"] + 16 * j, 16, 0, xh, xl, (a_free, A0["gates"] + j), (b_free, B0["gates"] + j), hook)
        o_turn(7, ost1, ps6, (p_e, 8))
        pe.wait_ge(o_lo, 8)
        pe.wait_ge(cl_ok, 1)

        def merge_pair(it, first):
            for c in range(8):
                if c == 0:
                    pe.wait_ge(a_free, it + A0["merge"])
                if c == 4 and first:
                    pe.wait_ge(b_free, B0["merge"])
                x_h, x_l, ps = (oh, ol, psA) if c < 4 else (ch, cl, psB)
                chunk(ps, x_h, x_l, (2 * (c % 4), 2 * (c % 4) + 1), c % 4 == 0, c % 4 == 3, C0["merge"] + c, 8, it)
                if c == 1 and not first:
                    group_t(it + (G0["merged"] - 1), st[:, 0, :, :], when=it + (G0["merged"] - 4))

        merge_pair(0, True)
        with pe.Fori(1, 4) as it:
            merge_pair(it, False)

        def need_last(g, c0):
            return lambda c: pe.wait_ge(tlo, g + 1) if c == c0 else None

        def post(g0):
            group_t(g0, hres[:, :, N * ORDER[0]:N * ORDER[0] + N], when=g0 - 3)

            def start(c):
                if c % 2 == 0 and c // 2 < 4:
                    i = c // 2
                    pe.wait_ge(tlo, g0 + i + 1)
                    if i < 3:
                        q = ORDER[i + 1]
                        group_t(g0 + i + 1, hres[:, :, N * q:N * q + N], when=g0 + i + 1 - 3)
            return start

        pair(C0["out1"], 16, 0, xh, xl, (a_free, A0["out1"]), None,
             lambda c: group_t(9, st[:, 0, :, :], when=6) if c == 1 else None, start=need_last(9, 6))
        pair(C0["out1"] + 16, 16, 0, xh, xl, (a_free, A0["out1"] + 1), (b_free, B0["out1"] + 1))

        pair(C0["ff1"], 16, 0, xh, xl, None, None, perm=PERM, start=post(G0["h1"]))
        with pe.Fori(1, 11) as it:
            pair(C0["ff1"], 16, it, xh, xl, (a_free, it + A0["ff1"]), None,
                 lambda c: group_t(it + (G0["f"] - 1), st[:, 0, :, :], when=it + (G0["f"] - 4)) if c == 1 else None,
                 perm=PERM)

        pair(C0["down1"], 44, 0, fh, fl, (a_free, A0["down1"]), None,
             lambda c: group_t(24, st[:, 0, :, :], when=21) if c == 1 else None, start=need_last(24, 20))
        pair(C0["down1"] + 44, 44, 0, fh, fl, (a_free, A0["down1"] + 1), (b_free, B0["down1"] + 1))

        pair(C0["latent"], 16, 0, xh, xl, None, None, perm=PERM, start=post(G0["h2"]))
        pe.wait_ge(lo_ready, C0["krope"] + 1)
        pe.wait_ge(o_lo, 8)
        s = C0["krope"] % 4
        for m in range(2):
            for k in range(16):
                w_h, w_l = hi[:, s, ROPE_B * k:ROPE_B * k + ROPE_B], lo[:, s, ROPE_B * k:ROPE_B * k + ROPE_B]
                dst = ps6[:, ROPE_B * m:ROPE_B * m + ROPE_B]
                nc.tensor.matmul(dst, xh[:, k, P * m:P * m + P], w_h, start=(k == 0), stop=False)
                nc.tensor.matmul(dst, xh[:, k, P * m:P * m + P], w_l, start=False, stop=False)
                ins = nc.tensor.matmul(dst, xl[:, k, P * m:P * m + P], w_h, start=False, stop=(k == 15))
        ins.then_inc(used, 1)

        def lat_hook(c):
            if c in (1, 3):
                i = c // 2
                group_t(G0["latent"] + i, st[:, i, :, :], when=G0["latent"] + i - 3)

        pair(C0["aq"], 16, 0, xh, xl, (tsrc, 26), (tsrc, 27), lat_hook, perm=PERM)
        pe.wait_ge(tlo, G0["latent"] + 2)
        for i in range(7):
            ps, free, f0 = (psA, a_free, A0["up_lat"]) if i % 2 == 0 else (psB, b_free, B0["up_lat"])
            pe.wait_ge(free, f0 + i // 2)
            k0 = 0 if i < 3 else 4
            for c in range(2):
                chunk(ps, lh, ll, (k0 + 2 * c, k0 + 2 * c + 1), c == 0, c == 1, C0["up_lat"] + 2 * i + c)

        pe.wait_ge(rot, 4)
        for m in range(2):
            ins = nc.tensor.transpose(psT[0:ROPE_B, 0, P * m:P * m + P], kr[:, m, :], ident[:])
        ins.then_inc(kr_t, 1)

        def heads_slot(slot):
            for n in head_steps(slot, 5):
                o_turn(n, ost2, psT[:, 0, T:2 * T], None)
            for n in head_steps(slot, 4):
                if n < 15:
                    pe.wait_ge(qk_e, n + 2)
                if n == 20:
                    pe.wait_ge(b_free, B0["akv"] + 2)
                if n < 16:
                    values(n, pt2, psT[:, 0, :], lambda k: ukv[:, k, 256 * (n - 8) + DH:256 * (n - 8) + 2 * DH],
                           (o_lo, n))
                else:
                    if n == 16:
                        pe.wait_ge(a_free, A0["akv"] + 2)
                    values(n, pt2, psT[:, 0, :], lambda k: aqkv[:, k, 2048 + DH * (n - 16):2048 + DH * (n - 15)],
                           (o_lo, n))
            for n in head_steps(slot, 3):
                p_turn(n, prob2, psT[:, 1, :], (p_e, n))
            for n in head_steps(slot, 1):
                scores(n, qkt2, (sm_ok, n), rope_=n < 16)
            for n in head_steps(slot, 0):
                if n == 8:
                    pe.wait_ge(b_free, B0["akv"])
                    pe.wait_ge(kr_e, 1)
                    pe.wait_ge(rot, 12)
                if n == 16:
                    pe.wait_ge(rot, 16)
                if n < 16:
                    h = n - 8
                    ins = qk_turn(n, lambda m: uq[:, m, 192 * h:192 * h + DH],
                                  lambda m: ukv[:, m, 256 * h:256 * h + DH], (qk_e, n))
                    if n == 8:
                        pe.wait_ge(krt_ok, 1)
                    pe.wait_ge(o_lo, n - 1)
                    for m in range(2):
                        ins = nc.tensor.transpose(psT[0:ROPE_B, 0, T + P * m:T + P * m + P],
                                                  uq[:, m, 192 * h + DH:192 * h + DH + ROPE_B], ident[:])
                else:
                    h = n - 16
                    ins = qk_turn(n, lambda m: aqkv[:, m, DH * h:DH * h + DH],
                                  lambda m: aqkv[:, m, 1024 + DH * h:1024 + DH * h + DH], (qk_e, n))
                ins.then_inc(qk_t, 1)

        for j in range(2):
            pair(C0["akv"] + 16 * j, 16, 0, xh, xl, (a_free, A0["akv"] + j), (b_free, B0["akv"] + j),
                    lambda c: heads_slot(16 * j + c), perm=PERM)

        frees = [(a_free, A0["out2"]), (b_free, B0["out2"]), (a_free, A0["out2"] + 1), (b_free, B0["out2"] + 1),
                 None, None, (a_free, A0["out2"] + 2), (b_free, B0["out2"] + 2)]
        for g, (j, bank, rows) in enumerate(OUT2):
            ps = (psA, psB)[bank]
            if frees[g] is not None:
                pe.wait_ge(*frees[g])
            if g == 0:
                pe.wait_ge(o_lo, 16)
            if g >= 6:
                for m in range(2):
                    nc.tensor.matmul(ps[:, m, :], ident[:], ukv[:, m, N * bank:N * bank + N], start=True, stop=False)
            for k in range(4):
                if g == 4:
                    pe.wait_ge(o_lo, 16 + 2 * k + 2)
                x_h, x_l = (lh, ll) if rows else (xh, xl)
                chunk(ps, x_h, x_l, (2 * k, 2 * k + 1), g < 4 and k == 0, g not in (2, 3) and k == 3,
                      C0["out2"] + 4 * g + k)
                if g < 4:
                    heads_slot(32 + 4 * g + k)

        for half, (up, dn, u) in enumerate((("up2a", "down2a", "u0"), ("up2b", "down2b", "u1"))):
            def up_hook(it, first):
                def hook(c):
                    if c == 1 and not first:
                        group_t(it * 2 + (G0[u] - 1), st[:, 1, :, :], when=it * 2 + (G0[u] - 4))
                    if c == 9:
                        group_t(it * 2 + G0[u], st[:, 0, :, :], when=it * 2 + (G0[u] - 3))
                return hook

            waits = (None, None) if half == 0 else ((a_free, A0[up]), (b_free, B0[up]))
            pair(C0[up], 16, 0, xh, xl, *waits, up_hook(0, True), perm=PERM, start=post(G0["h3"]) if half == 0 else None)
            with pe.Fori(1, 4) as it:
                pair(C0[up], 16, it, xh, xl, (a_free, it + A0[up]), (b_free, it + B0[up]), up_hook(it, False), perm=PERM)
            g = G0[u] + 7
            pair(C0[dn], 32, 0, uh, ul, (a_free, A0[dn]), (b_free, B0[dn]),
                 lambda c: group_t(g, st[:, 1, :, :], when=g - 3) if c == 1 else None, start=need_last(g, 14))
            pair(C0[dn] + 32, 32, 0, uh, ul,
                    (a_free, A0[dn] + 1) if half == 0 else (acc_ok, 1),
                    (b_free, B0[dn] + 1) if half == 0 else (acc_ok, 2))
    ctx.close()


def shape_constants():
    import numpy as np

    w, c = np.arange(64)[:, None], np.arange(64)[None, :]
    start = np.clip(w - 8, 0, 48)
    window = (c >= start) & (c < start + 16)
    q, k = np.arange(T)[:, None], np.arange(T)[None, :]
    causal = k <= q
    count = (causal & (q - k <= 128)).astype(int) + (causal & ((q - k) % 4 == 0)) + (causal & ((q - k) % 16 == 0))
    theta = 500000.0
    freq = [theta ** (-2.0 * i / ROPE_B) for i in range(32)] + [theta ** (-2.0 * i / ROPE_A) for i in range(16)]
    return {
        "ident": np.eye(P, dtype=np.float32),
        "mask_na": np.tile(np.where(window, 0.0, -1e30), (2, 1)).astype(np.float32),
        "log_count": np.where(count > 0, np.log(np.maximum(count, 1)), -1e30).astype(np.float32),
        "causal": np.where(causal, 0.0, -1e30).astype(np.float32),
        "inv_freq": np.asarray(freq, dtype=np.float32),
    }


def kernel(**inputs):
    import numpy as _np
    import concourse.bacc as _bacc
    from concourse import mybir as _mybir
    from concourse.bass_utils import run_bass_kernel_spmd as _run

    nc = _bacc.Bacc("TRN2", target_bir_lowering=False, num_devices=1)
    arrays, aps = {}, {}
    for name, array in {**inputs, **shape_constants()}.items():
        arr = _np.ascontiguousarray(array)
        if name in ("mix_post_g", "ffn_post_g", "norm_attn_post_2", "norm_mlp_post_2"):
            arr = arr.reshape(-1)
        arrays[f"in_{name}"] = arr
        aps[name] = nc.dram_tensor(f"in_{name}", arr.shape, _mybir.dt.from_np(arr.dtype), kind="ExternalInput").ap()
    out = nc.dram_tensor("out_0", (1, T, D), _mybir.dt.float32, kind="ExternalOutput").ap()
    build(nc, aps, out)
    r = _run(nc, [arrays], core_ids=[0])
    return r.results[0]["out_0"]
```
